# Optimizing a Trainium2 kernel written in Bass

```python
import jax, jax.numpy as jnp
from jax import lax
import numpy as np

D_MODEL = 1024
BATCH = 1
SEQ = 256
DEPTH = 2

CHUNK = 64
Q_BLOCK = 128
EPS = 1e-6
N_MOD = 6

MLA_HEADS = 8
MLA_NOPE = 64
MLA_ROPE = 32
MLA_V = 64
Q_LORA = 256
KV_LORA = 128
ROPE_BASE = 10000.0

SB_HEADS = 8
SB_HEAD_DIM = 64

MLA_WIDTH = MLA_HEADS * MLA_V
SB_WIDTH = SB_HEADS * SB_HEAD_DIM
MIX_WIDTH = MLA_WIDTH + SB_WIDTH
IN_COLS = Q_LORA + KV_LORA + MLA_ROPE + 3 * SB_WIDTH
SPLIT_POINTS = (Q_LORA, Q_LORA + KV_LORA, Q_LORA + KV_LORA + MLA_ROPE,
                Q_LORA + KV_LORA + MLA_ROPE + SB_WIDTH,
                Q_LORA + KV_LORA + MLA_ROPE + 2 * SB_WIDTH)

D_FF = 2560
N_EXPERTS = 8
TOP_K = 2
D_FF_EXPERT = 3584
N_DENSE = (DEPTH + 1) // 2
N_MOE = DEPTH // 2

kernel_name = 'hymba_mla_stickbreaking_moe_adaln_chunk_causal'

def rms_norm(x, g):
    xf = x.astype(jnp.float32)
    y = xf * lax.rsqrt(jnp.mean(xf * xf, axis=-1, keepdims=True) + EPS)
    return (y * g.astype(jnp.float32)).astype(x.dtype)

def apply_rotary(x, cos, sin):
    half = x.shape[-1] // 2
    x1, x2 = x[..., :half], x[..., half:]
    cos = cos.astype(x.dtype)
    sin = sin.astype(x.dtype)
    return jnp.concatenate([x1 * cos - x2 * sin, x2 * cos + x1 * sin], axis=-1)

def swiglu(x, w_gate, w_up, w_down):
    return (jax.nn.silu(x @ w_gate) * (x @ w_up)) @ w_down

def sweep_query_blocks(q, block_fn):
    b, h, s, dq = q.shape
    nb = s // Q_BLOCK
    qb = jnp.moveaxis(q.reshape(b, h, nb, Q_BLOCK, dq), 2, 0)
    out = lax.map(lambda args: block_fn(args[0], args[1]), (qb, jnp.arange(nb)))
    return jnp.moveaxis(out, 0, 2).reshape(b, h, s, out.shape[-1])

def mla_attention(q, k, v):
    scale = (MLA_NOPE + MLA_ROPE) ** -0.5
    key_chunk = jnp.arange(k.shape[2]) // CHUNK

    def block(qblk, i):
        q_chunk = (i * Q_BLOCK + jnp.arange(Q_BLOCK)) // CHUNK
        allowed = key_chunk[None, :] <= q_chunk[:, None]
        logits = jnp.einsum('bhqd,bhkd->bhqk', qblk, k,
                            preferred_element_type=jnp.float32) * scale
        logits = jnp.where(allowed, logits, -jnp.inf)
        p = jax.nn.softmax(logits, axis=-1)
        return jnp.einsum('bhqk,bhkd->bhqd', p.astype(v.dtype), v)

    return sweep_query_blocks(q, block)

def stick_breaking_attention(q, k, v):
    scale = SB_HEAD_DIM ** -0.5
    key_idx = jnp.arange(k.shape[2])

    def block(qblk, i):
        q_idx = i * Q_BLOCK + jnp.arange(Q_BLOCK)
        strict = key_idx[None, :] < q_idx[:, None]
        z = jnp.einsum('bhqd,bhkd->bhqk', qblk, k,
                       preferred_element_type=jnp.float32) * scale
        log_keep = jnp.where(strict, jax.nn.log_sigmoid(-z), 0.0)
        key_axis = log_keep.ndim - 1
        log_stick = lax.cumsum(log_keep, axis=key_axis, reverse=True) - log_keep
        a = jnp.where(strict, jnp.exp(jax.nn.log_sigmoid(z) + log_stick), 0.0)
        return jnp.einsum('bhqk,bhkd->bhqd', a.astype(v.dtype), v)

    return sweep_query_blocks(q, block)

def token_mixer(h, cos, sin, w_in, g_q_lat, w_uq, g_kv_lat, w_ukv, g_grp_mla, g_grp_sb, w_out):
    b, s, _ = h.shape
    proj = h @ w_in
    c_q, c_kv, k_rope, q_sb, k_sb, v_sb = jnp.split(proj, SPLIT_POINTS, axis=-1)

    q = (rms_norm(c_q, g_q_lat) @ w_uq).reshape(b, s, MLA_HEADS, MLA_NOPE + MLA_ROPE)
    q_nope = q[..., :MLA_NOPE]
    q_rope = apply_rotary(q[..., MLA_NOPE:], cos[:, :, None, :], sin[:, :, None, :])
    kv = (rms_norm(c_kv, g_kv_lat) @ w_ukv).reshape(b, s, MLA_HEADS, MLA_NOPE + MLA_V)
    k_nope, v_mla = kv[..., :MLA_NOPE], kv[..., MLA_NOPE:]
    k_rope = apply_rotary(k_rope, cos, sin)
    q_mla = jnp.concatenate([q_nope, q_rope], axis=-1)
    k_mla = jnp.concatenate(
        [k_nope, jnp.broadcast_to(k_rope[:, :, None, :], (b, s, MLA_HEADS, MLA_ROPE))], axis=-1)
    o_mla = mla_attention(q_mla.transpose(0, 2, 1, 3), k_mla.transpose(0, 2, 1, 3),
                          v_mla.transpose(0, 2, 1, 3))
    o_mla = o_mla.transpose(0, 2, 1, 3).reshape(b, s, MLA_WIDTH)

    def heads(t):
        return t.reshape(b, s, SB_HEADS, SB_HEAD_DIM).transpose(0, 2, 1, 3)
    o_sb = stick_breaking_attention(heads(q_sb), heads(k_sb), heads(v_sb))
    o_sb = o_sb.transpose(0, 2, 1, 3).reshape(b, s, SB_WIDTH)

    merged = jnp.concatenate([rms_norm(o_mla, g_grp_mla), rms_norm(o_sb, g_grp_sb)], axis=-1)
    return merged @ w_out

def moe_swiglu(h, w_router, b_router, w_gate, w_up, w_down):
    b, s, d = h.shape
    t = h.reshape(b * s, d)
    logits = (t @ w_router + b_router).astype(jnp.float32)
    top_vals, top_idx = lax.top_k(logits, TOP_K)
    top_w = jax.nn.softmax(top_vals, axis=-1)
    combine = jnp.sum(jax.nn.one_hot(top_idx, N_EXPERTS, dtype=jnp.float32) * top_w[..., None],
                      axis=1).astype(t.dtype)
    out = jnp.zeros_like(t)
    for e in range(N_EXPERTS):
        out = out + combine[:, e:e + 1] * swiglu(t, w_gate[e], w_up[e], w_down[e])
    return out.reshape(b, s, d)

def setup_inputs(seed: int = 0) -> dict:
    key = jax.random.key(seed)
    ks = jax.random.split(key, 24)
    f32 = jnp.float32

    def nrm(k, shape, scale):
        return jax.random.normal(k, shape, f32) * scale

    def gain(k, shape):
        return 1.0 + 0.1 * jax.random.normal(k, shape, f32)

    offset = jax.random.randint(ks[2], (BATCH, 1), 0, 64) * CHUNK
    positions = (offset + jnp.arange(SEQ, dtype=jnp.int32)[None, :]).astype(jnp.int32)
    return {
        'x': nrm(ks[0], (BATCH, SEQ, D_MODEL), 1.0),
        'c': nrm(ks[1], (BATCH, D_MODEL), 1.0),
        'positions': positions,
        'w_ada': nrm(ks[3], (DEPTH, D_MODEL, N_MOD * D_MODEL), 0.5 * D_MODEL ** -0.5),
        'b_ada': nrm(ks[4], (DEPTH, N_MOD * D_MODEL), 0.02),
        'g_mix': gain(ks[5], (DEPTH, D_MODEL)),
        'g_ffn': gain(ks[6], (DEPTH, D_MODEL)),
        'w_in': nrm(ks[7], (DEPTH, D_MODEL, IN_COLS), D_MODEL ** -0.5),
        'g_q_lat': gain(ks[8], (DEPTH, Q_LORA)),
        'w_uq': nrm(ks[9], (DEPTH, Q_LORA, MLA_HEADS * (MLA_NOPE + MLA_ROPE)), Q_LORA ** -0.5),
        'g_kv_lat': gain(ks[10], (DEPTH, KV_LORA)),
        'w_ukv': nrm(ks[11], (DEPTH, KV_LORA, MLA_HEADS * (MLA_NOPE + MLA_V)), KV_LORA ** -0.5),
        'g_grp_mla': gain(ks[12], (DEPTH, MLA_WIDTH)),
        'g_grp_sb': gain(ks[13], (DEPTH, SB_WIDTH)),
        'w_out': nrm(ks[14], (DEPTH, MIX_WIDTH, D_MODEL), MIX_WIDTH ** -0.5),
        'w_ff_gate': nrm(ks[15], (N_DENSE, D_MODEL, D_FF), D_MODEL ** -0.5),
        'w_ff_up': nrm(ks[16], (N_DENSE, D_MODEL, D_FF), D_MODEL ** -0.5),
        'w_ff_down': nrm(ks[17], (N_DENSE, D_FF, D_MODEL), D_FF ** -0.5),
        'w_router': nrm(ks[18], (N_MOE, D_MODEL, N_EXPERTS), D_MODEL ** -0.5),
        'b_router': nrm(ks[19], (N_MOE, N_EXPERTS), 0.01),
        'w_ex_gate': nrm(ks[20], (N_MOE, N_EXPERTS, D_MODEL, D_FF_EXPERT), D_MODEL ** -0.5),
        'w_ex_up': nrm(ks[21], (N_MOE, N_EXPERTS, D_MODEL, D_FF_EXPERT), D_MODEL ** -0.5),
        'w_ex_down': nrm(ks[22], (N_MOE, N_EXPERTS, D_FF_EXPERT, D_MODEL), D_FF_EXPERT ** -0.5),
        'g_final': gain(ks[23], (D_MODEL,)),
    }

def reference(x, c, positions, w_ada, b_ada, g_mix, g_ffn, w_in, g_q_lat, w_uq, g_kv_lat,
              w_ukv, g_grp_mla, g_grp_sb, w_out, w_ff_gate, w_ff_up, w_ff_down, w_router,
              b_router, w_ex_gate, w_ex_up, w_ex_down, g_final):
    half = MLA_ROPE // 2
    inv_freq = ROPE_BASE ** (-jnp.arange(half, dtype=jnp.float32) / half)
    ang = positions.astype(jnp.float32)[..., None] * inv_freq
    cos, sin = jnp.cos(ang), jnp.sin(ang)
    c_act = jax.nn.silu(c)

    for layer in range(DEPTH):
        mod = c_act @ w_ada[layer] + b_ada[layer]
        shift_m, scale_m, gate_m, shift_f, scale_f, gate_f = [
            m[:, None, :] for m in jnp.split(mod, N_MOD, axis=-1)]

        h = rms_norm(x, g_mix[layer]) * (1.0 + scale_m) + shift_m
        mixed = token_mixer(h, cos, sin, w_in[layer], g_q_lat[layer], w_uq[layer],
                            g_kv_lat[layer], w_ukv[layer], g_grp_mla[layer], g_grp_sb[layer],
                            w_out[layer])
        x = x + gate_m * mixed

        h = rms_norm(x, g_ffn[layer]) * (1.0 + scale_f) + shift_f
        if layer % 2 == 0:
            i = layer // 2
            y = swiglu(h, w_ff_gate[i], w_ff_up[i], w_ff_down[i])
        else:
            i = layer // 2
            y = moe_swiglu(h, w_router[i], b_router[i], w_ex_gate[i], w_ex_up[i], w_ex_down[i])
        x = x + gate_f * y

    return rms_norm(x, g_final)


_drawn_inputs = setup_inputs


def setup_inputs(seed=0):
    import zlib

    import numpy as np

    out = dict(_drawn_inputs(seed))
    spreads = {}
    factors = {'g_q_lat': 3.918, 'b_router': 7.861}
    for name, (base, spread) in spreads.items():
        noise = np.random.default_rng([zlib.crc32(name.encode()), seed]).standard_normal(out[name].shape)
        drawn = base * np.exp(spread * noise) if base else spread * noise
        out[name] = __import__('jax').numpy.asarray(drawn.astype(out[name].dtype))
    for name, factor in factors.items():
        out[name] = (out[name] * factor).astype(out[name].dtype)
    return out
```

```python
from contextlib import ExitStack
from itertools import islice

import numpy as np

import concourse.bass as bass
from concourse import mybir

ALU = mybir.AluOpType
ACT = mybir.ActivationFunctionType
AX = mybir.AxisListType
F32 = mybir.dt.float32
F32R = mybir.dt.float32r
I32 = mybir.dt.int32
U32 = mybir.dt.uint32

P = 128
EPS = 1e-6
CHUNK = 64
MASKED = -1e30
ROPE_BASE = 10000.0
EXP_LN = "natural_log_exp_and_others"
ABSENT = 4096.0
RAW = 7
SPLIT = 3
UNIT = 2048

TURN = (6.28125, float(np.float32(0.0019350051879882812)), float(2 * np.pi - 6.28125 - 0.0019350051879882812))
ROUND = 12582912.0
PI_IN = 3.1415925


def trunk_kernel(nc, x_in, c_in, positions, w_ada, b_ada, g_mix, g_ffn, w_in, g_q_lat, w_uq, g_kv_lat,
                 w_ukv, g_grp_mla, g_grp_sb, w_out, w_ff_gate, w_ff_up, w_ff_down, w_router, b_router,
                 w_ex_gate, w_ex_up, w_ex_down, g_final, out):
    L, D, _ = w_ada.shape
    T = x_in.shape[1]
    G = T // P
    KD = D // P
    QL, KVL = g_q_lat.shape[1], g_kv_lat.shape[1]
    MW, SW = g_grp_mla.shape[1], g_grp_sb.shape[1]
    HD = 64
    H = SW // HD
    QW = w_uq.shape[2] // H
    RO = QW - HD
    RH = RO // 2
    LAT = QL + KVL + RO
    FF = w_ff_gate.shape[2]
    E, FE = w_ex_gate.shape[1], w_ex_gate.shape[3]
    FC, EC = FF // 512, FE // 512
    assert (L, G, KD, H, E) == (2, 2, 8, 8, 8) and MW == H * HD and KVL == P and QL == 2 * P

    stream = []
    ends = {}

    def end(name, use):
        ends[name] = sum(s[3] == use for s in stream)

    def k_rows(w, half, c0, n):
        return w[half * 512:(half + 1) * 512, c0:c0 + n].rearrange("(k p) n -> p k n", p=P)

    def add_ada(l, c, half):
        stream.append((k_rows(w_ada[l], half, c * 512, 512), 4, 512, "dve"))

    def add_cols(name, w, c0, n):
        for half in range(2):
            stream.append((k_rows(w, half, c0, n), 4, n, "split"))
        end(name, "split")

    def add_ff(kind, c, half):
        if kind == "down":
            r0 = c * 512 + half * 256
            stream.append((w_ff_down[0][r0:r0 + 256, :].rearrange("(k p) n -> p k n", p=P), 2, 1024, "split"))
        else:
            w = w_ff_gate if kind == "gate" else w_ff_up
            stream.append((k_rows(w[0], half, c * 512, 512), 4, 512, "split"))
        if half == 1:
            end((kind, c), "split")

    def ffn_order(chunks):
        o = []
        for c in range(chunks):
            o += [("gate", c, 0), ("gate", c, 1), ("up", c, 0), ("up", c, 1)]
            if c > 0:
                o += [("down", c - 1, 0), ("down", c - 1, 1)]
        return o + [("down", chunks - 1, 0), ("down", chunks - 1, 1)]

    order = ffn_order(EC)
    ff_order = ffn_order(FC)

    chunks = [(0, c) for c in range(12)] + [(1, c) for c in (0, 1, 2, 3, 6, 7, 8, 9, 4, 5, 10, 11)]
    RINGED = 10
    ada_units = [(l, c, half) for l, c in chunks for half in range(2)]
    FF_FIRST = 3
    ff_ada = {j: 1 for j in range(FF_FIRST, len(ff_order))}
    ff_ada[6] = 2

    for u in ada_units[:8]:
        add_ada(*u)
    for l in range(L):
        ada = iter(ada_units[8:2 * RINGED] if l == 0 else ())

        def add_next_ada(n):
            for u in islice(ada, n):
                add_ada(*u)

        def add_half(w, c0, n, half):
            stream.append((k_rows(w, half, c0, n), 4, n, "split"))

        add_cols(("lat", l), w_in[l], 0, LAT)
        add_cols(("v", l), w_in[l], LAT + 2 * SW, SW)
        add_next_ada(1)
        for half in range(2):
            add_half(w_in[l], LAT, SW, half)
            add_next_ada(1)
        end(("q", l), "split")
        stream.append((w_uq[l].rearrange("(k p) n -> p k n", p=P), 2, H * QW, "pe"))
        end(("uq", l), "pe")
        add_half(w_in[l], LAT + SW, SW, 0)
        add_next_ada(1)
        stream.append((w_ukv[l].rearrange("(k p) n -> p k n", p=P), 1, 2 * MW, "pe"))
        end(("ukv", l), "pe")
        add_half(w_in[l], LAT + SW, SW, 1)
        end(("k", l), "split")
        add_next_ada(1)
        for c in range(2):
            for half in range(2):
                add_half(w_out[l], c * 512, 512, half)
                if (c, half) == (0, 0):
                    add_next_ada(1)
                if (c, half) == (1, 0):
                    add_next_ada(6)
            end(("out", l, c), "split")
        if l == 0:
            n_ff = len(stream)
            done = 2 * RINGED
            for j, u in enumerate(ff_order):
                add_ff(*u)
                for _ in range(ff_ada.get(j, 0)):
                    add_ada(*ada_units[done])
                    done += 1
            assert done == len(ada_units)
    N0 = len(stream)
    split_at = {}
    counts = {"split": 0, "pe": 0, "dve": 0}
    for n, s in enumerate(stream):
        split_at[n] = counts[s[3]]
        counts[s[3]] += 1
    units_of = {use: [n for n, s in enumerate(stream) if s[3] == use] for use in counts}
    S0 = counts["split"]
    NU = len(order)
    at = {u: j for j, u in enumerate(order)}

    def sb_heads(i):
        return [i, i + 2, i + 4, i + 6] if i < 2 else [4 * ((i - 2) // 2) + (i - 2) % 2 + a for a in (0, 2)]

    assert NU % RAW == 0 and NU % SPLIT == 0

    with ExitStack() as ctx:
        def sb(name, shape, dt=F32, where=None):
            return (where or ctx).enter_context(nc.sbuf_tensor(name, shape, dt))

        def sem(name):
            return ctx.enter_context(nc.semaphore(name))

        bank = [ctx.enter_context(nc.psum_tensor(f"bank{i}", [P, 512], F32)) for i in range(8)]

        raw = sb("raw", [P, RAW, UNIT])
        w_hi = sb("w_hi", [P, SPLIT, UNIT], F32R)
        w_lo = sb("w_lo", [P, SPLIT, UNIT], F32R)
        x = sb("x", [P, G, D])
        y = sb("y", [P, G, D])
        gate_m = sb("gate_m", [P, D])
        gate_f = sb("gate_f", [P, D])
        early = ExitStack()
        q_t = sb("q_t", [QW, H, T], where=early)
        k_t = sb("k_t", [QW, H, T], where=early)
        early.close()
        h_hi = sb("h_hi", [P, KD, T], F32R)
        h_lo = sb("h_lo", [P, KD, T], F32R)
        ident = sb("ident", [P, P])
        ones = sb("ones", [P, P])
        from_here = sb("from_here", [P, P])
        before = sb("before", [P, P])
        strict = sb("strict", [P, T])
        chunked = sb("chunked", [P, T])
        slot_no = sb("slot_no", [P, P])
        rows1 = sb("rows1", [P, P])
        rows2 = sb("rows2", [P, P])
        cols1 = sb("cols1", [P, P])
        cols2 = sb("cols2", [P, 32])
        mod = sb("mod", [P, L, 2, 2, KD])
        modt = sb("modt", [P, 2, KD])
        squares = sb("squares", [P, 4])
        rstd = sb("rstd", [P, 4])
        cos2 = sb("cos2", [P, G, 1, RO])
        sin2 = sb("sin2", [P, G, 1, RO])
        ring_sum = sb("ring_sum", [P, 2, 512])

        final_gain = sb("final_gain", [P, D])
        wr = sb("wr", [P, KD, E])
        br = sb("br", [P, E])

        over = ExitStack()
        lat = sb("lat", [P, G, LAT], where=over)
        lat_t = sb("lat_t", [P, 3, T], where=over)
        v_sb = sb("v_sb", [P, G, SW], where=over)
        q_sbt = sb("q_sbt", [P, 4, T], where=over)
        k_sbt = sb("k_sbt", [P, 4, T], where=over)
        v_mla = sb("v_mla", [P, G, MW], where=over)
        probs = sb("probs", [P, 2, 512], where=over)
        probs_t = sb("probs_t", [P, 2, 512], where=over)
        neg_max = sb("neg_max", [P, 2 * H], where=over)
        sums = sb("sums", [P, 2 * H], where=over)
        recip = sb("recip", [P, 2 * H], where=over)
        rot = sb("rot", [P, 2, G, H, RO], where=over)
        rot_a, rot_b = rot[:, 0], rot[:, 1]
        sticks = rot[:, :, :, :, :].rearrange("p i g h c -> p i (g h c)")
        here = ExitStack()
        q_tok = sb("q_tok", [P, G, H, QW], where=here)
        k_tok = sb("k_tok", [P, G, H, QW], where=here)
        here.close()
        sub = ExitStack()
        zm = sb("zm", [P, 3, 512], where=sub)
        keep = sb("keep", [P, 4, 512], where=sub)
        sub.close()
        hf = sb("hf", [P, KD, T], where=over)
        over.close()
        ffn = ExitStack()
        act = sb("act", [P, 4, T], where=ffn)
        a_hi = sb("a_hi", [P, 2, 4, T], F32R, where=ffn)
        a_lo = sb("a_lo", [P, 2, 4, T], F32R, where=ffn)
        norm_only = ExitStack()
        hfn = sb("hfn", [P, KD, T], where=norm_only)
        norm_only.close()
        ff_sum = sb("ff_sum", [P, len(chunks) - RINGED, 512], where=ffn)
        ffn.close()
        moe = ExitStack()
        hfm = sb("hfm", [P, KD, T], where=moe)
        e_act = sb("e_act", [P, 512], where=moe)
        e_hi = sb("e_hi", [P, 2, 4, P], F32R, where=moe)
        e_lo = sb("e_lo", [P, 2, 4, P], F32R, where=moe)
        hgf = sb("hgf", [P, KD, P], where=moe)
        hg_hi = sb("hg_hi", [P, KD, P], F32R, where=moe)
        hg_lo = sb("hg_lo", [P, KD, P], F32R, where=moe)
        y_e = sb("y_e", [P, D], where=moe)
        acc = sb("acc", [P, G, D], where=moe)
        sel = sb("sel", [P, G, P], where=moe)
        sel_w = sb("sel_w", [P, G, P], where=moe)
        sel_wt = sb("sel_wt", [P, T], where=moe)
        logits = sb("logits", [P, G, E], where=moe)
        top = sb("top", [P, G, 8], where=moe)
        topi = sb("topi", [P, G, 8], U32, where=moe)
        topf = sb("topf", [P, G, 8], where=moe)
        hot = sb("hot", [P, G, 2, E], where=moe)
        tw = sb("tw", [P, G, 4], where=moe)
        chosen = sb("chosen", [P, G, E], where=moe)
        comb = sb("comb", [P, G, E], where=moe)
        place = sb("place", [P, 2 * E + 1, 4], where=moe)
        now = sb("now", [P, 4], where=moe)
        full = sb("full", [P, 1], where=moe)
        full_i = sb("full_i", [P, 1], I32, where=moe)
        moe.close()
        pre = ExitStack()
        pos_i = sb("pos_i", [P, G], I32, where=pre)
        pos_f = sb("pos_f", [P, G], where=pre)
        freq = sb("freq", [P, RH], where=pre)
        ang = sb("ang", [P, G, RH], where=pre)
        turns = sb("turns", [P, 2, G, RH], where=pre)
        rest = sb("rest", [P, 2, G, RH], where=pre)
        trig = sb("trig", [P, 2, G, RH], where=pre)
        pre.close()

        unit_in = [sem(f"unit_in{i}") for i in range(RAW)]
        small_in = sem("small_in"); pos_in = sem("pos_in"); x_in_s = sem("x_in_s")
        bias_in = sem("bias_in"); router_in = sem("router_in"); final_in = sem("final_in")
        hi_done = sem("hi_done"); lo_done = sem("lo_done")
        split_used = sem("split_used"); plain_used = sem("plain_used")
        consts = sem("consts"); c_silu = sem("c_silu"); cols_tp = sem("cols_tp"); cols_done = sem("cols_done")
        angles = sem("angles"); trig_done = sem("trig_done"); trig2 = sem("trig2")
        vec_used = sem("vec_used"); crossed = sem("crossed"); mod_done = sem("mod_done"); gate_done = sem("gate_done")
        sq_done = sem("sq_done"); var_done = sem("var_done"); rstd_done = sem("rstd_done"); y_done = sem("y_done")
        h_tp = sem("h_tp"); hf_done = sem("hf_done"); h_done = sem("h_done")
        proj = sem("proj"); lat_done = sem("lat_done"); vsb_done = sem("vsb_done"); qk_done = sem("qk_done")
        z_ready = sem("z_ready"); zm_done = sem("zm_done"); ln_done = sem("ln_done"); keep_done = sem("keep_done")
        cs_ready = sem("cs_ready"); w_done = sem("w_done"); stick_done = sem("stick_done"); pv_done = sem("pv_done")
        osb_done = sem("osb_done")
        latn_done = sem("latn_done"); lat_tp = sem("lat_tp"); latt_done = sem("latt_done")
        kv_act = sem("kv_act"); qtok_done = sem("qtok_done"); vmla_done = sem("vmla_done"); qkrot_done = sem("qkrot_done")
        qk_tp = sem("qk_tp"); qt_act = sem("qt_act"); qt_dve = sem("qt_dve")
        s_ready = sem("s_ready"); max_done = sem("max_done"); p_done = sem("p_done"); p_tp = sem("p_tp")
        pt_done = sem("pt_done"); mpv_done = sem("mpv_done"); omla_done = sem("omla_done")
        mixed = sem("mixed"); x_done = sem("x_done")
        g_ready = sem("g_ready"); u_ready = sem("u_ready"); silu_done = sem("silu_done"); a_done = sem("a_done"); ff_ready = sem("ff_ready")
        lg_ready = sem("lg_ready"); rd_done = sem("rd_done"); re_done = sem("re_done"); ch_done = sem("ch_done"); pos_ready = sem("pos_ready")
        place_done = sem("place_done")
        sel_done = sem("sel_done"); hg_ready = sem("hg_ready"); hgf_done = sem("hgf_done"); hg_done = sem("hg_done")
        sw_tp = sem("sw_tp"); sw_done = sem("sw_done")
        eg_ready = sem("eg_ready"); eu_ready = sem("eu_ready"); esilu = sem("esilu"); ea_done = sem("ea_done")
        e_tp = sem("e_tp"); ehi_done = sem("ehi_done"); elo_done = sem("elo_done"); ed_ready = sem("ed_ready")
        ye_done = sem("ye_done"); sc_ready = sem("sc_ready"); acc_done = sem("acc_done")
        fin_acc = sem("fin_acc"); ye_end = sem("ye_end"); sc_end = sem("sc_end"); acc_end = sem("acc_end"); fin_x = sem("fin_x"); fin_y = sem("fin_y"); out_done = sem("out_done")
        act_own = sem("act_own"); dve_own = sem("dve_own"); pool_own = sem("pool_own")

        ONE_LAYER = 3
        block = ctx.enter_context(nc.Block())

        def unit_view(n):
            _, k, cols, _ = stream[n]
            return raw[:, n % RAW, 0:k * cols].rearrange("p (k n) -> p k n", k=k)

        def unit_wait(eng, n):
            eng.wait_ge(unit_in[n % RAW], 16 * (n // RAW + 1))

        @block.sync
        def _(sp):
            def load(n):
                if n >= RAW:
                    old = n - RAW
                    sp.wait_ge({"split": lo_done, "pe": plain_used, "dve": vec_used}[stream[old][3]], split_at[old] + 1)
                sp.dma_start(unit_view(n), stream[n][0]).then_inc(unit_in[n % RAW], 16)

            r1 = b_ada.rearrange("l (r p) -> (l r) p", p=P)
            nb = L * 6 * KD
            sp.dma_start(rows2[0:8, :], c_in.rearrange("b (r p) -> (b r) p", p=P)).then_inc(small_in, 16)
            sp.dma_start(rows2[8:12, :], g_q_lat.rearrange("l (r p) -> (l r) p", p=P)).then_inc(small_in, 16)
            sp.dma_start(rows2[12:14, :], g_kv_lat).then_inc(small_in, 16)
            sp.dma_start(rows2[14:22, :], g_grp_mla.rearrange("l (r p) -> (l r) p", p=P)).then_inc(small_in, 16)
            sp.dma_start(rows2[22:30, :], g_grp_sb.rearrange("l (r p) -> (l r) p", p=P)).then_inc(small_in, 16)
            sp.dma_start(rows1[0:nb, :], r1).then_inc(small_in, 16)
            sp.dma_start(rows1[nb:nb + 16, :], g_mix.rearrange("l (r p) -> (l r) p", p=P)).then_inc(small_in, 16)
            sp.dma_start(rows1[nb + 16:nb + 32, :], g_ffn.rearrange("l (r p) -> (l r) p", p=P)).then_inc(small_in, 16)
            for n in range(2):
                load(n)
            sp.dma_start(x[:, :, :], x_in[0].rearrange("(g p) d -> p g d", p=P)).then_inc(x_in_s, 16)
            with nc.allow_non_contiguous_dma(reason="256 positions, one to a partition"):
                sp.dma_start(pos_i[:, :], positions[0].rearrange("(g p) -> p g", p=P)).then_inc(pos_in, 16)
            bias = lambda l, part: b_ada[l:l + 1, part * D:(part + 1) * D].to_broadcast([P, D])
            for n in range(2, N0):
                if n == 10:
                    for part, t in ((2, gate_m), (5, gate_f)):
                        sp.dma_start(t[:, :], bias(0, part)).then_inc(bias_in, 16)
                if n == n_ff + 8:
                    sp.wait_ge(x_done, 4)
                    sp.dma_start(gate_m[:, :], bias(1, 2)).then_inc(bias_in, 16)
                    sp.wait_ge(crossed, RINGED)
                    sp.dma_start(ring_sum[:, :, :].rearrange("p a n -> p (a n)"), bias(1, 5)).then_inc(bias_in, 16)
                load(n)
            def load_expert(q, e):
                for j, (kind, c, half) in enumerate(order):
                    slot = (N0 + j) % RAW
                    sp.wait_ge(lo_done, q * NU + (S0 + j - RAW + 1))
                    if kind == "down":
                        r0 = c * 512 + half * 256
                        src = w_ex_down[0, bass.ds(e, 1), r0:r0 + 256, :].rearrange("o (k p) n -> p (o k) n", p=P)
                        dst = raw[:, slot, :].rearrange("p (k n) -> p k n", k=2)
                    else:
                        w = w_ex_gate if kind == "gate" else w_ex_up
                        src = w[0, bass.ds(e, 1), half * 512:(half + 1) * 512, c * 512:(c + 1) * 512].rearrange(
                            "o (k p) n -> p (o k) n", p=P)
                        dst = raw[:, slot, :].rearrange("p (k n) -> p k n", k=4)
                    sp.dma_start(dst, src).then_inc(unit_in[slot], 16)

            sp.dma_start(final_gain[:, :], g_final.rearrange("(o d) -> o d", o=1).to_broadcast([P, D])).then_inc(final_in, 16)
            sp.dma_start(wr[:, :, :], w_router[0].rearrange("(k p) e -> p k e", p=P)).then_inc(router_in, 16)
            sp.dma_start(br[:, :], b_router[0:1, :].to_broadcast([P, E])).then_inc(router_in, 16)
            sp.wait_ge(plain_used, counts["pe"])
            with sp.Fori(0, E) as q:
                load_expert(q, q)
            sp.wait_ge(place_done, 1)
            more = sp.value_load(full_i[0:1, 0:1])
            with sp.If(more > P):
                with sp.Fori(0, E) as e:
                    load_expert(e + E, e)
            sp.wait_ge(fin_y, 2)
            sp.dma_start(out[0].rearrange("(g p) d -> p g d", p=P), y[:, :, :]).then_inc(out_done, 16)
            sp.wait_ge(out_done, 16)

        @block.gpsimd
        def _(pool):
            n = 0
            for t in (ident, from_here, before, chunked, strict, ones, slot_no):
                if t is slot_no:
                    pool.iota(t[:, :], pattern=[[1, P]], base=0, channel_multiplier=0,
                              allow_small_or_imprecise_dtypes=True).then_inc(pool_own, 1)
                else:
                    pool.memset(t[:, :], 1.0 if t in (ones, from_here, before) else 0.0).then_inc(pool_own, 1)
                n += 1
            for i in range(RH):
                f = float(np.float32(np.power(np.float32(ROPE_BASE), np.float32(-i / RH))))
                pool.memset(freq[:, i:i + 1], f).then_inc(pool_own, 1)
                n += 1
            pool.wait_ge(pool_own, n)
            pool.affine_select(out=ident[:, :], in_=ident[:, :], compare_op=ALU.not_equal, fill=1.0, base=0,
                               pattern=[[-1, P]], channel_multiplier=1).then_inc(consts, 1)
            pool.affine_select(out=from_here[:, :], in_=from_here[:, :], compare_op=ALU.is_ge, fill=0.0, base=0,
                               pattern=[[-1, P]], channel_multiplier=1).then_inc(consts, 1)
            pool.affine_select(out=before[:, :], in_=before[:, :], compare_op=ALU.is_gt, fill=0.0, base=0,
                               pattern=[[1, P]], channel_multiplier=-1).then_inc(consts, 1)
            pool.affine_select(out=strict[:, 0:P], in_=strict[:, 0:P], compare_op=ALU.is_gt, fill=MASKED, base=0,
                               pattern=[[1, P]], channel_multiplier=-1).then_inc(consts, 1)
            pool.memset(chunked[0:CHUNK, P + CHUNK:2 * P], MASKED).then_inc(consts, 1)

        @block.scalar
        def _(act_e):
            own = [0]

            def link(ins):
                ins.then_inc(act_own, 1)
                own[0] += 1
                act_e.wait_ge(act_own, own[0])

            def hi(s):
                n = units_of["split"][s]
                words = stream[n][1] * stream[n][2]
                unit_wait(act_e, n)
                if s >= SPLIT:
                    act_e.wait_ge(split_used, s - SPLIT + 1)
                act_e.activation(w_hi[:, s % SPLIT, 0:words], raw[:, n % RAW, 0:words], ACT.Copy).then_inc(hi_done, 1)

            def rstd_of(m, n):
                act_e.wait_ge(var_done, m + 1)
                link(act_e.activation(rstd[:, 0:n], squares[:, 0:n], ACT.Ln))
                act_e.activation(rstd[:, 0:n], rstd[:, 0:n], ACT.Exp, scale=-0.5).then_inc(rstd_done, 1)

            def evacuate(m, dst, gain, shift):
                for k in range(KD):
                    if k % 2 == 0:
                        act_e.wait_ge(h_tp, 4 * m + k // 2 + 1)
                    src = bank[k // 2][:, (k % 2) * T:(k % 2 + 1) * T]
                    if shift is None:
                        act_e.activation(dst[:, k, :], src, ACT.Copy, scale=gain(k)).then_inc(hf_done, 1)
                    else:
                        act_e.activation(dst[:, k, :], src, ACT.Identity, bias=shift(k), scale=gain(k)).then_inc(hf_done, 1)

            act_e.wait_ge(small_in, 16 * 8)
            act_e.activation(rows2[0:8, :], rows2[0:8, :], ACT.Silu).then_inc(c_silu, 1)
            act_e.wait_ge(angles, 1)
            act_e.activation(trig[:, :, :, :], rest[:, :, :, :], ACT.Sin).then_inc(trig_done, 1)
            s = 0
            for l in range(L):
                act_e.preload_act_table_set(EXP_LN)
                m = ONE_LAYER * l
                gcol = lambda i: (lambda k, i=i: mod[:, l, i, 1, k:k + 1])
                scol = lambda i: (lambda k, i=i: mod[:, l, i, 0, k:k + 1])
                if l == 0:
                    act_e.wait_ge(x_in_s, 16)
                else:
                    act_e.wait_ge(x_done, 8)
                for g in range(G):
                    act_e.activation(y[:, g, :], x[:, g, :], ACT.Square, accum_out=squares[:, g:g + 1]).then_inc(sq_done, 1)
                rstd_of(4 * l, G)
                for _ in range(3):
                    hi(s); s += 1
                act_e.wait_ge(mod_done, 4 * l + 2)
                evacuate(m, hf, gcol(0), scol(0))
                hi(s); s += 1
                hi(s); s += 1
                act_e.wait_ge(split_used, ends["lat", l])
                for g in range(G):
                    act_e.activation(lat[:, g, :], bank[g][:, 0:LAT], ACT.Copy).then_inc(lat_done, 1)
                act_e.wait_ge(lat_done, 2 * (l + 1))
                for g in range(G):
                    act_e.activation(y[:, g, 0:QL], lat[:, g, 0:QL], ACT.Square,
                                     accum_out=squares[:, g:g + 1]).then_inc(sq_done, 1)
                    act_e.activation(y[:, g, QL:QL + KVL], lat[:, g, QL:QL + KVL], ACT.Square,
                                     accum_out=squares[:, 2 + g:3 + g]).then_inc(sq_done, 1)
                hi(s); s += 1
                rstd_of(4 * l + 1, 4)
                act_e.wait_ge(split_used, ends["v", l])
                for g in range(G):
                    act_e.activation(v_sb[:, g, :], bank[2 + g][:, :], ACT.Copy).then_inc(vsb_done, 1)
                hi(s); s += 1
                hi(s); s += 1
                act_e.wait_ge(lat_tp, 2 * l + 2)
                for b in range(3):
                    col = 8 + 2 * l + b if b < 2 else 12 + l
                    src = bank[0][:, b * T:(b + 1) * T] if b < 2 else bank[1][:, 0:T]
                    act_e.activation(lat_t[:, b, :], src, ACT.Copy, scale=cols2[:, col:col + 1]).then_inc(latt_done, 1)
                act_e.wait_ge(plain_used, ends["uq", l])
                for g in range(G):
                    bq = 2 if g == 0 else 0
                    act_e.activation(q_tok[:, g, 0:5, :], bank[bq][:, 0:5 * QW].rearrange("p (h c) -> p h c", c=QW),
                                     ACT.Copy, scale=float(QW) ** -0.5).then_inc(qtok_done, 1)
                    act_e.activation(q_tok[:, g, 5:8, :], bank[bq + 1][:, 0:3 * QW].rearrange("p (h c) -> p h c", c=QW),
                                     ACT.Copy, scale=float(QW) ** -0.5).then_inc(qtok_done, 1)
                hi(s); s += 1
                act_e.wait_ge(plain_used, ends["ukv", l])
                for i in range(2):
                    kv = bank[2 + i][:, :].rearrange("p (h c) -> p h c", c=P)
                    act_e.activation(k_tok[:, 0, 4 * i:4 * i + 4, 0:HD], kv[:, :, 0:HD], ACT.Copy).then_inc(kv_act, 1)
                    act_e.activation(v_mla[:, 0, i * 256:(i + 1) * 256].rearrange("p (h c) -> p h c", c=HD),
                                     kv[:, :, HD:P], ACT.Copy).then_inc(kv_act, 1)
                hi(s); s += 1
                hi(s); s += 1
                for i in range(0, 8, 2):
                    act_e.wait_ge(qk_tp, 8 * l + i + 1)
                    dst = (q_t if i < 4 else k_t)[:, 2 * (i % 4):2 * (i % 4) + 2, :]
                    act_e.activation(dst, bank[(4 + i) % 8][0:QW, :].rearrange("p (h t) -> p h t", t=T),
                                     ACT.Copy).then_inc(qt_act, 1)

                for i in range(6 + 2):
                    if i < 6:
                        t = 6 * l + i
                        kb = keep[:, i if i < 2 else 2 + i % 2, :]
                        act_e.wait_ge(zm_done, t + 1)
                        if i >= 4:
                            act_e.wait_ge(cs_ready, t - 1)
                        link(act_e.activation(kb, zm[:, i % 3, :], ACT.Abs))
                        link(act_e.activation(kb, kb, ACT.Exp, scale=-1.0))
                        act_e.activation(kb, kb, ACT.Ln, bias=1.0).then_inc(ln_done, 1)
                        act_e.wait_ge(max_done, t + 1)
                        heads = 4 if i < 2 else 2
                        w = 512 // heads
                        c0 = 4 * i if i < 2 else H + 2 * (i - 2)
                        for h in range(heads):
                            pr = probs[:, i % 2, h * w:(h + 1) * w]
                            act_e.activation(pr, pr, ACT.Exp, bias=neg_max[:, c0 + h:c0 + h + 1],
                                             accum_out=sums[:, c0 + h:c0 + h + 1]).then_inc(p_done, 1)
                    if i >= 2:
                        j = i - 2
                        t = 6 * l + j
                        act_e.wait_ge(w_done, t + 1)
                        if j >= 2:
                            act_e.wait_ge(pv_done, t - 1)
                        act_e.activation(sticks[:, j % 2, :], zm[:, j % 3, :], ACT.Exp).then_inc(stick_done, 1)
                act_e.wait_ge(omla_done, 2 * (l + 1))
                act_e.wait_ge(osb_done, 2 * (l + 1))
                for g in range(G):
                    for i in range(2):
                        act_e.activation(hf[:, 4 * g + 2 * i:4 * g + 2 * i + 2, :], y[:, g, i * 512:(i + 1) * 512].rearrange("p (a b) -> p a b", a=2),
                                         ACT.Square, accum_out=squares[:, 2 * g + i:2 * g + i + 1]).then_inc(sq_done, 1)
                rstd_of(4 * l + 2, 4)
                evacuate(m + 1, hf, lambda k: cols2[:, (14 + 4 * l + k if k < 4 else 22 + 4 * l + k - 4):][:, 0:1], None)
                hi(s); s += 1
                if l == 0:
                    for _ in range(3):
                        hi(s); s += 1
                act_e.wait_ge(x_done, 8 * l + 4)
                for g in range(G):
                    act_e.activation(y[:, g, :], x[:, g, :], ACT.Square, accum_out=squares[:, g:g + 1]).then_inc(sq_done, 1)
                rstd_of(4 * l + 3, G)
                act_e.wait_ge(mod_done, 4 * l + 4)
                evacuate(m + 2, hfn if l == 0 else hfm, gcol(1), scol(1))
                if l == 0:
                    for j, (kind, c, half) in enumerate(ff_order):
                        if j >= FF_FIRST:
                            hi(s); s += 1
                        if (kind, half) == ("up", 1):
                            act_e.wait_ge(split_used, ends["gate", c])
                            if c > 0:
                                act_e.wait_ge(a_done, 2 * c)
                            for i in range(2):
                                act_e.activation(act[:, 2 * i:2 * i + 2, :], bank[i][:, :].rearrange("p (k t) -> p k t", t=T),
                                                 ACT.Silu).then_inc(silu_done, 1)

            act_e.wait_ge(rd_done, 1)
            act_e.activation(tw[:, :, 1], tw[:, :, 0], ACT.Exp).then_inc(re_done, 1)

            def evacuate_rows(done):
                for i in range(2):
                    act_e.activation(y_e[:, i * 512:(i + 1) * 512], bank[4 + i][:, :], ACT.Copy).then_inc(done, 1)

            def evacuate_gathered(q, half):
                act_e.wait_ge(hg_ready, q + 1)
                for k in range(4 * half, 4 * half + 4):
                    act_e.activation(hgf[:, k, :], bank[6 + k // 4][:, (k % 4) * P:(k % 4 + 1) * P], ACT.Identity,
                                     bias=mod[:, 1, 1, 0, k:k + 1], scale=mod[:, 1, 1, 1, k:k + 1]).then_inc(hgf_done, 1)

            def evacuate_weights(q):
                act_e.wait_ge(sw_tp, q + 1)
                act_e.activation(sel_wt[:, :], bank[3][:, 0:T], ACT.Copy).then_inc(sw_done, 1)

            def expert(q):
                def hi_e(j):
                    act_e.wait_ge(unit_in[(N0 + j) % RAW], q * (16 * NU // RAW) + 16 * ((N0 + j) // RAW + 1))
                    act_e.wait_ge(split_used, q * NU + (S0 + j - SPLIT + 1))
                    act_e.activation(w_hi[:, (S0 + j) % SPLIT, :], raw[:, (N0 + j) % RAW, :], ACT.Copy).then_inc(hi_done, 1)

                def silu(c):
                    act_e.wait_ge(split_used, q * NU + (S0 + at["gate", c, 1] + 1))
                    act_e.activation(e_act[:, :], bank[0][:, :], ACT.Silu).then_inc(esilu, 1)

                def high_t(c):
                    act_e.wait_ge(e_tp, q * EC + (c + 1))
                    act_e.activation(e_hi[:, c % 2, :, :], bank[2][:, :].rearrange("p (k t) -> p k t", t=P),
                                     ACT.Copy).then_inc(ehi_done, 1)

                for j, (kind, c, half) in enumerate(order):
                    hi_e(j)
                    if (kind, c, half) == ("gate", 0, 1):
                        act_e.wait_ge(split_used, q * NU + S0)
                        evacuate_rows(ye_done)
                    if (kind, half) == ("up", 1):
                        if c > 0:
                            high_t(c - 1)
                        silu(c)
                    if (kind, c, half) == ("up", EC - 1, 0):
                        evacuate_gathered(q + 1, 0)
                        evacuate_gathered(q + 1, 1)
                    if (kind, c, half) == ("gate", 1, 0):
                        evacuate_weights(q)
                    if (kind, c, half) == ("down", EC - 1, 0):
                        high_t(EC - 1)

            act_e.preload_act_table(ACT.Silu)
            evacuate_gathered(0, 0)
            evacuate_gathered(0, 1)
            with act_e.Fori(0, E) as q:
                expert(q)
            act_e.wait_ge(place_done, 1)
            more = act_e.value_load(full_i[0:1, 0:1])
            with act_e.If(more > P):
                with act_e.Fori(E, 2 * E) as q:
                    expert(q)
                act_e.wait_ge(split_used, S0 + 2 * E * NU)
            act_e.wait_ge(split_used, S0 + E * NU)
            evacuate_rows(ye_end)
            act_e.preload_act_table_set(EXP_LN)
            act_e.wait_ge(fin_x, 1)
            for g in range(G):
                act_e.activation(y[:, g, :], x[:, g, :], ACT.Square, accum_out=squares[:, g:g + 1]).then_inc(sq_done, 1)
            rstd_of(4 * L, G)

        @block.vector
        def _(dve):
            own = [0]

            def link(ins):
                ins.then_inc(dve_own, 1)
                own[0] += 1
                dve.wait_ge(dve_own, own[0])

            def lo(s):
                n = units_of["split"][s]
                words = stream[n][1] * stream[n][2]
                dve.wait_ge(hi_done, s + 1)
                dve.tensor_tensor(w_lo[:, s % SPLIT, 0:words], raw[:, n % RAW, 0:words],
                                  w_hi[:, s % SPLIT, 0:words].bitcast(F32), ALU.subtract).then_inc(lo_done, 1)

            nsq = [0]

            def variance(cols):
                nsq[0] += {2: 2, 4: 4}[cols[-1][1]]
                dve.wait_ge(sq_done, nsq[0])
                for i, (a, b, w) in enumerate(cols):
                    ins = dve.tensor_scalar(squares[:, a:b], squares[:, a:b], 1.0 / w, EPS, ALU.mult, ALU.add)
                    if i + 1 < len(cols):
                        link(ins)
                ins.then_inc(var_done, 1)

            def split_operand(m, src):
                for j in range(4):
                    dve.wait_ge(hf_done, 8 * m + 2 * j + 2)
                    part = slice(2 * j, 2 * j + 2)
                    dve.tensor_copy(h_hi[:, part, :], src[:, part, :]).then_inc(h_done, 1)
                    dve.wait_ge(h_done, 8 * m + 2 * j + 1)
                    dve.tensor_tensor(h_lo[:, part, :], src[:, part, :], h_hi[:, part, :].bitcast(F32),
                                      ALU.subtract).then_inc(h_done, 1)

            def normalise(m, norm, ny):
                dve.wait_ge(rstd_done, norm + 1)
                for g in range(G):
                    dve.tensor_scalar(y[:, g, :], x[:, g, :], rstd[:, g:g + 1], None, ALU.mult).then_inc(y_done, 1)

            def mod_shift(l, i, b, c0):
                p0 = l * 48 + 24 * i
                dve.tensor_tensor(mod[:, l, i, 0, :], bank[b][:, c0:c0 + KD], cols1[:, p0:p0 + KD], ALU.add).then_inc(mod_done, 1)

            def mod_gain(l, i, b, c0):
                p0 = l * 48 + 24 * i + KD
                gcol = 96 + 16 * i + 8 * l
                link(dve.tensor_tensor(modt[:, i, :], bank[b][:, c0:c0 + KD], cols1[:, p0:p0 + KD], ALU.add))
                dve.scalar_tensor_tensor(out=mod[:, l, i, 1, :], in0=modt[:, i, :], scalar=1.0,
                                         in1=cols1[:, gcol:gcol + KD], op0=ALU.add, op1=ALU.mult).then_inc(mod_done, 1)

            def gate_half(b, r, gate, half, bias, biases):
                dve.wait_ge(crossed, r + 1)
                dve.wait_ge(bias_in, 16 * biases)
                c = slice(half * 512, (half + 1) * 512)
                dve.tensor_tensor(gate[:, c], bias, bank[b][:, :], ALU.add).then_inc(gate_done, 1)

            vec = [0]

            def sum_unit():
                n = units_of["dve"][vec[0]]
                r, half = vec[0] // 2, vec[0] % 2
                vec[0] += 1
                w = unit_view(n)
                unit_wait(dve, n)
                if r < RINGED:
                    dst = ring_sum[:, r % 2, :]
                    if r >= 2 and half == 0:
                        dve.wait_ge(crossed, r - 1)
                else:
                    dst = ff_sum[:, r - RINGED, :]
                for k in range(4):
                    ck = cols2[:, 4 * half + k:4 * half + k + 1]
                    if half == 0 and k == 0:
                        ins = dve.tensor_scalar(dst, w[:, k, :], ck, None, ALU.mult)
                    else:
                        ins = dve.scalar_tensor_tensor(out=dst, in0=w[:, k, :], scalar=ck, in1=dst, op0=ALU.mult, op1=ALU.add)
                    if k < 3:
                        link(ins)
                ins.then_inc(vec_used, 1)
                if half == 0:
                    dve.wait_ge(vec_used, vec[0])

            def add_gated(gate, ready, product):
                for c in range(2):
                    for g in range(G):
                        i = 2 * c + g
                        dve.wait_ge(split_used, ready[c])
                        cs = slice(c * 512, (c + 1) * 512)
                        link(dve.tensor_tensor(product(i % 2), bank[4 + i][:, :], gate[:, cs], ALU.mult))
                        dve.tensor_tensor(x[:, g, cs], x[:, g, cs], product(i % 2), ALU.add).then_inc(x_done, 1)

            dve.wait_ge(cols_tp, 1)
            dve.tensor_copy(cols1[:, :], bank[0][:, 0:P]).then_inc(cols_done, 1)
            dve.tensor_copy(cols2[:, 0:30], bank[0][:, P:P + 30]).then_inc(cols_done, 1)
            dve.wait_ge(cols_done, 2)
            for _ in range(8):
                sum_unit()
            dve.wait_ge(pos_in, 16)
            dve.wait_ge(pool_own, 7 + RH)
            link(dve.tensor_copy(pos_f[:, :], pos_i[:, :]))
            for g in range(G):
                link(dve.tensor_scalar(ang[:, g, :], freq[:, :], pos_f[:, g:g + 1], None, ALU.mult))
            link(dve.tensor_scalar(turns[:, 0, :, :], ang[:, :, :], 1.0 / (2 * np.pi), None, ALU.mult))
            link(dve.tensor_scalar(turns[:, 1, :, :], turns[:, 0, :, :], 0.25, None, ALU.add))
            link(dve.tensor_scalar(turns[:, :, :, :], turns[:, :, :, :], ROUND, None, ALU.add))
            link(dve.tensor_scalar(turns[:, :, :, :], turns[:, :, :, :], -ROUND, None, ALU.add))
            for i in range(2):
                for j, part in enumerate(TURN):
                    src = ang[:, :, :] if j == 0 else rest[:, i, :, :]
                    link(dve.scalar_tensor_tensor(out=rest[:, i, :, :], in0=turns[:, i, :, :], scalar=-part, in1=src,
                                                  op0=ALU.mult, op1=ALU.add))
            link(dve.tensor_scalar(rest[:, 1, :, :], rest[:, 1, :, :], float(np.pi / 2), None, ALU.add))
            dve.tensor_scalar(rest[:, :, :, :], rest[:, :, :, :], PI_IN, -PI_IN, ALU.min, ALU.max).then_inc(angles, 1)
            dve.wait_ge(trig_done, 1)
            for i in range(2):
                half = slice(i * RH, (i + 1) * RH)
                dve.tensor_copy(cos2[:, :, 0, half], trig[:, 1, :, :]).then_inc(trig2, 1)
                dve.tensor_scalar(sin2[:, :, 0, half], trig[:, 0, :, :], -1.0 if i == 0 else 1.0, None, ALU.mult).then_inc(trig2, 1)

            s = 0
            for l in range(L):
                m = ONE_LAYER * l
                if l == 0:
                    dve.wait_ge(crossed, 4)
                    mod_shift(0, 0, 3, 0)
                    mod_gain(0, 0, 3, KD)
                variance([(0, 2, D)])
                normalise(m, 4 * l, 0)
                for _ in range(3):
                    lo(s); s += 1
                split_operand(m, hf)
                for _ in range(2):
                    lo(s); s += 1
                    if l == 0:
                        sum_unit()
                variance([(0, 2, QL), (2, 4, KVL)])
                dve.wait_ge(rstd_done, 4 * l + 2)
                if l == 0:
                    dve.wait_ge(trig2, 4)
                for g in range(G):
                    dve.tensor_scalar(lat[:, g, 0:QL], lat[:, g, 0:QL], rstd[:, g:g + 1], None, ALU.mult).then_inc(latn_done, 1)
                    dve.tensor_scalar(lat[:, g, QL:QL + KVL], lat[:, g, QL:QL + KVL], rstd[:, 2 + g:3 + g], None,
                                      ALU.mult).then_inc(latn_done, 1)
                lo(s); s += 1
                if l == 0:
                    sum_unit()
                for g in range(G):
                    kr = lat[:, g, QL + KVL:LAT]
                    ra, rb = rot_a[:, g, 0, :], rot_b[:, g, 0, :]
                    link(dve.tensor_tensor(ra, kr, cos2[:, g, 0, :], ALU.mult))
                    link(dve.tensor_tensor(rb[:, 0:RH], kr[:, RH:RO], sin2[:, g, 0, 0:RH], ALU.mult))
                    link(dve.tensor_tensor(rb[:, RH:RO], kr[:, 0:RH], sin2[:, g, 0, RH:RO], ALU.mult))
                    link(dve.tensor_tensor(kr, ra, rb, ALU.add))
                for g in range(G):
                    dve.tensor_copy(k_tok[:, g, :, HD:QW],
                                    lat[:, g, QL + KVL:LAT].rearrange("p (o c) -> p o c", o=1).to_broadcast([P, H, RO])
                                    ).then_inc(qkrot_done, 1)
                lo(s); s += 1
                if l == 0:
                    sum_unit()
                    gate_half(6, 4, gate_m, 0, gate_m[:, 0:512], 2)

                def out_of_psum(i):
                    dve.wait_ge(split_used, ends["q" if i < 2 else "k", l])
                    dst = (q_sbt if i < 2 else k_sbt)[:, 2 * (i % 2):2 * (i % 2) + 2, :]
                    dve.tensor_scalar(dst, bank[4 + i][:, :].rearrange("p (a t) -> p a t", t=T),
                                      HD ** -0.5 if i < 2 else 1.0, None, ALU.mult).then_inc(qk_done, 1)

                out_of_psum(0)
                out_of_psum(1)
                if l == 0:
                    gate_half(7, 5, gate_m, 1, gate_m[:, 512:1024], 2)
                lo(s); s += 1
                if l == 0:
                    sum_unit()
                dve.wait_ge(qtok_done, 4 * (l + 1))
                for g in range(G):
                    qr = q_tok[:, g, :, HD:QW]
                    cb = cos2[:, g, :, :].to_broadcast([P, H, RO])
                    sb0 = sin2[:, g, :, 0:RH].to_broadcast([P, H, RH])
                    sb1 = sin2[:, g, :, RH:RO].to_broadcast([P, H, RH])
                    dve.tensor_tensor(rot_b[:, g, :, 0:RH], qr[:, :, RH:RO], sb0, ALU.mult).then_inc(dve_own, 1)
                    dve.tensor_tensor(rot_b[:, g, :, RH:RO], qr[:, :, 0:RH], sb1, ALU.mult).then_inc(dve_own, 1)
                    own[0] += 2
                    link(dve.tensor_tensor(rot_a[:, g, :, :], qr, cb, ALU.mult))
                    dve.tensor_tensor(qr, rot_a[:, g, :, :], rot_b[:, g, :, :], ALU.add).then_inc(qkrot_done, 1)
                lo(s); s += 1
                if l == 0:
                    sum_unit()
                dve.wait_ge(plain_used, ends["ukv", l])
                for i in range(2):
                    kv = bank[i][:, :].rearrange("p (h c) -> p h c", c=P)
                    dve.tensor_copy(k_tok[:, 1, 4 * i:4 * i + 4, 0:HD], kv[:, :, 0:HD]).then_inc(qkrot_done, 1)
                    dve.tensor_copy(v_mla[:, 1, i * 256:(i + 1) * 256].rearrange("p (h c) -> p h c", c=HD),
                                    kv[:, :, HD:P]).then_inc(vmla_done, 1)
                lo(s); s += 1
                out_of_psum(2)
                out_of_psum(3)
                for i in range(1, 8, 2):
                    dve.wait_ge(qk_tp, 8 * l + i + 1)
                    dst = (q_t if i < 4 else k_t)[:, 2 * (i % 4):2 * (i % 4) + 2, :]
                    dve.tensor_copy(dst, bank[(4 + i) % 8][0:QW, :].rearrange("p (h t) -> p h t", t=T)).then_inc(qt_dve, 1)
                lo(s); s += 1

                for i in range(6 + 2):
                    if i < 6:
                        t = 6 * l + i
                        dve.wait_ge(z_ready, t + 1)
                        if i >= 3:
                            dve.wait_ge(stick_done, t - 2)
                        w = P if i < 2 else T
                        n = 512 // w
                        dve.tensor_tensor(zm[:, i % 3, :].rearrange("p (h q) -> p h q", q=w),
                                          bank[0][:, :].rearrange("p (h q) -> p h q", q=w),
                                          strict[:, 0:w].rearrange("p (o q) -> p o q", o=1).to_broadcast([P, n, w]),
                                          ALU.add).then_inc(zm_done, 1)
                        dve.wait_ge(s_ready, t + 1)
                        if i >= 2:
                            dve.wait_ge(p_tp, t - 1)
                        heads = 4 if i < 2 else 2
                        w = 512 // heads
                        c0 = 4 * i if i < 2 else H + 2 * (i - 2)
                        pr = probs[:, i % 2, :].rearrange("p (h k) -> p h k", k=w)
                        mk = chunked[:, T - w:T].rearrange("p (o k) -> p o k", o=1).to_broadcast([P, heads, w])
                        link(dve.tensor_tensor(pr, bank[4][:, :].rearrange("p (h k) -> p h k", k=w), mk, ALU.add))
                        dve.tensor_reduce(neg_max[:, c0:c0 + heads], pr, AX.X, ALU.max, negate=True).then_inc(max_done, 1)
                    if 1 <= i <= 6:
                        j = i - 1
                        t = 6 * l + j
                        dve.wait_ge(ln_done, t + 1)
                        kb = keep[:, j if j < 2 else 2 + j % 2, :]
                        dve.scalar_tensor_tensor(out=kb, in0=zm[:, j % 3, :], scalar=0.0, in1=kb, op0=ALU.max,
                                                 op1=ALU.add).then_inc(keep_done, 1)
                    if i >= 2:
                        j = i - 2
                        t = 6 * l + j
                        dve.wait_ge(cs_ready, t + 1)
                        dve.tensor_tensor(zm[:, j % 3, :], zm[:, j % 3, :], bank[1][:, :],
                                          ALU.subtract).then_inc(w_done, 1)
                    if l == 0 and i < 6:
                        sum_unit()
                    if l == 0 and i == 3:
                        dve.wait_ge(crossed, 8)
                        mod_shift(0, 1, 7, 0)
                    if 1 <= i <= 6:
                        j = i - 1
                        t = 6 * l + j
                        dve.wait_ge(p_tp, t + 1)
                        if j >= 2:
                            dve.wait_ge(mpv_done, t - 1)
                        dve.tensor_copy(probs_t[:, j % 2, :], bank[5][:, :]).then_inc(pt_done, 1)
                if l == 0:
                    dve.wait_ge(crossed, 10)
                    mod_gain(0, 1, 0, 0)
                dve.wait_ge(p_done, 16 * (l + 1))
                link(dve.reciprocal(recip[:, :], sums[:, :]))
                dve.wait_ge(mpv_done, 6 * (l + 1))
                for g in range(G):
                    dve.tensor_tensor(y[:, g, 0:MW].rearrange("p (h c) -> p h c", c=HD),
                                      bank[6 + g][:, :].rearrange("p (h c) -> p h c", c=HD),
                                      recip[:, g * H:(g + 1) * H].rearrange("p (h o) -> p h o", o=1).to_broadcast([P, H, HD]),
                                      ALU.mult).then_inc(omla_done, 1)
                dve.wait_ge(pv_done, 6 * (l + 1))
                for g in range(G):
                    dve.tensor_copy(y[:, g, MW:], bank[2 + g][:, :]).then_inc(osb_done, 1)
                variance([(0, 4, MW)])
                dve.wait_ge(rstd_done, 4 * l + 3)
                for g in range(G):
                    for i in range(2):
                        part = y[:, g, i * 512:(i + 1) * 512]
                        dve.tensor_scalar(part, part, rstd[:, 2 * g + i:2 * g + i + 1], None, ALU.mult).then_inc(y_done, 1)
                split_operand(m + 1, hf)
                lo(s); s += 1
                if l == 0:
                    for _ in range(2):
                        lo(s); s += 1
                dve.wait_ge(gate_done, 2 if l == 0 else 6)
                add_gated(gate_m, (ends["out", l, 0], ends["out", l, 1]), lambda i: probs[:, i, :])
                if l == 0:
                    lo(s); s += 1
                variance([(0, 2, D)])
                normalise(m + 2, 4 * l + 3, 0)
                if l == 0:
                    split_operand(m + 2, hfn)
                    def gated_ff(c):
                        dve.wait_ge(silu_done, 2 * c + 2)
                        dve.wait_ge(split_used, ends["up", c])
                        for i in range(2):
                            link(dve.tensor_tensor(act[:, 2 * i:2 * i + 2, :], act[:, 2 * i:2 * i + 2, :],
                                                   bank[2 + i][:, :].rearrange("p (k t) -> p k t", t=T), ALU.mult))
                        if c >= 2:
                            dve.wait_ge(split_used, ends["down", c - 2])
                        dve.tensor_copy(a_hi[:, c % 2, :, :], act[:, :, :]).then_inc(a_done, 1)
                        dve.wait_ge(a_done, 2 * c + 1)
                        dve.tensor_tensor(a_lo[:, c % 2, :, :], act[:, :, :], a_hi[:, c % 2, :, :].bitcast(F32),
                                          ALU.subtract).then_inc(a_done, 1)

                    for j, (kind, c, half) in enumerate(ff_order):
                        if j >= FF_FIRST:
                            lo(s); s += 1
                        for _ in range(ff_ada.get(j, 0)):
                            sum_unit()
                        if (kind, c, half) == ("gate", 1, 1):
                            gated_ff(0)
                        if (kind, half) == ("down", 1) and c + 1 < FC:
                            gated_ff(c + 1)
                    for half in range(2):
                        gate_half(half, 10 + half, gate_f, half, gate_f[:, half * 512:(half + 1) * 512], 2)
                    dve.wait_ge(gate_done, 4)
                    add_gated(gate_f, (ends["down", FC - 1],) * 2,
                              lambda i: act[:, 2 * i:2 * i + 2, :].rearrange("p a t -> p (a t)"))
                    for half, b in enumerate((3, 0)):
                        gate_half(b, 20 + half, gate_m, half, gate_m[:, half * 512:(half + 1) * 512], 4)
                    for i in range(2):
                        mod_shift(1, i, 2, 2 * KD * i)
                        mod_gain(1, i, 2, 2 * KD * i + KD)
                    for half, b in enumerate((1, 3)):
                        gate_half(b, 22 + half, gate_f, half, ring_sum[:, half, :], 4)

            dve.wait_ge(router_in, 32)
            dve.wait_ge(lg_ready, 1)
            for g in range(G):
                link(dve.tensor_tensor(logits[:, g, :], bank[4][:, g * E:(g + 1) * E], br[:, :], ALU.add))
                link(dve.max(top[:, g, :], logits[:, g, :]))
                link(dve.max_index(topi[:, g, :], top[:, g, :], logits[:, g, :]))
            link(dve.tensor_copy(topf[:, :, :], topi[:, :, :]))
            dve.tensor_tensor(tw[:, :, 0], top[:, :, 1], top[:, :, 0], ALU.subtract).then_inc(rd_done, 1)
            for g in range(G):
                for i in range(2):
                    link(dve.tensor_scalar(hot[:, g, i, :], slot_no[:, 0:E], topf[:, g, i:i + 1], None, ALU.is_equal))
                dve.tensor_tensor(chosen[:, g, :], hot[:, g, 0, :], hot[:, g, 1, :], ALU.add).then_inc(ch_done, 1)
            dve.wait_ge(re_done, 1)
            link(dve.tensor_scalar(tw[:, :, 2], tw[:, :, 1], 1.0, None, ALU.add))
            link(dve.reciprocal(tw[:, :, 2], tw[:, :, 2]))
            link(dve.tensor_tensor(tw[:, :, 3], tw[:, :, 1], tw[:, :, 2], ALU.mult))
            for g in range(G):
                link(dve.tensor_scalar(comb[:, g, :], hot[:, g, 0, :], tw[:, g, 2:3], None, ALU.mult))
                link(dve.scalar_tensor_tensor(out=comb[:, g, :], in0=hot[:, g, 1, :], scalar=tw[:, g, 3:4],
                                              in1=comb[:, g, :], op0=ALU.mult, op1=ALU.add))
            dve.wait_ge(pos_ready, 1)
            link(dve.memset(place[:, 2 * E, :], ABSENT))
            for g in range(G):
                link(dve.scalar_tensor_tensor(out=place[:, 0:E, g], in0=chosen[:, g, :], scalar=-ABSENT,
                                              in1=bank[5][:, g * E:(g + 1) * E], op0=ALU.mult, op1=ALU.add))
                link(dve.tensor_scalar(place[:, E:2 * E, g], place[:, 0:E, g], ABSENT - P, None, ALU.add))
                link(dve.tensor_scalar(place[:, 0:E, g], place[:, 0:E, g], ABSENT, None, ALU.add))
                link(dve.tensor_copy(place[:, 0:E, 2 + g], comb[:, g, :]))
                link(dve.tensor_copy(place[:, E:2 * E, 2 + g], comb[:, g, :]))
            link(dve.tensor_reduce(full[:, :], bank[5][:, 2 * E:3 * E], AX.X, ALU.max))
            link(dve.memset(acc[:, :, :], 0.0))
            dve.memset(sel_wt[:, :], 0.0).then_inc(sw_done, 1)
            dve.tensor_copy(full_i[:, :], full[:, :]).then_inc(place_done, 1)

            PER = 1

            def select(q, n):
                dve.tensor_copy(now[:, :], place[:, bass.ds(q, 1), :]).then_inc(dve_own, 1)
                dve.wait_ge(dve_own, n)
                for g in range(G):
                    dve.tensor_scalar(sel[:, g, :], slot_no[:, :], now[:, g:g + 1], None, ALU.is_equal).then_inc(sel_done, 1)
                    dve.tensor_scalar(sel_w[:, g, :], slot_no[:, :], now[:, g:g + 1], now[:, 2 + g:3 + g], ALU.is_equal,
                                      ALU.mult).then_inc(sel_done, 1)

            def add_rows(i, done):
                g, half = i // 2, i % 2
                a = acc[:, g, half * 512:(half + 1) * 512]
                dve.tensor_tensor(a, a, bank[6 + i % 2][:, :], ALU.add).then_inc(done, 1)

            def split_gathered(q):
                for i in range(2):
                    dve.wait_ge(hgf_done, q * KD + (4 * i + 4))
                    part = slice(4 * i, 4 * i + 4)
                    dve.tensor_copy(hg_hi[:, part, :], hgf[:, part, :]).then_inc(hg_done, 1)
                    dve.wait_ge(hg_done, q * 4 + (2 * i + 1))
                    dve.tensor_tensor(hg_lo[:, part, :], hgf[:, part, :], hg_hi[:, part, :].bitcast(F32),
                                      ALU.subtract).then_inc(hg_done, 1)

            base = own[0]
            dve.wait_ge(place_done, 1)
            select(0, base + 1)
            split_gathered(0)

            def expert(q):
                def lo_e(j):
                    dve.wait_ge(hi_done, q * NU + (S0 + j + 1))
                    sl = (S0 + j) % SPLIT
                    dve.tensor_tensor(w_lo[:, sl, :], raw[:, (N0 + j) % RAW, :], w_hi[:, sl, :].bitcast(F32),
                                      ALU.subtract).then_inc(lo_done, 1)

                def gated(c):
                    dve.wait_ge(esilu, q * EC + (c + 1))
                    dve.wait_ge(split_used, q * NU + (S0 + at["up", c, 1] + 1))
                    dve.tensor_tensor(e_act[:, :], e_act[:, :], bank[1][:, :], ALU.mult).then_inc(ea_done, 1)

                def low_t(c):
                    dve.wait_ge(ehi_done, q * EC + (c + 1))
                    dve.tensor_tensor(e_lo[:, c % 2, :, :], bank[2][:, :].rearrange("p (k t) -> p k t", t=P),
                                      e_hi[:, c % 2, :, :].bitcast(F32), ALU.subtract).then_inc(elo_done, 1)

                for j, (kind, c, half) in enumerate(order):
                    lo_e(j)
                    if (kind, c, half) == ("up", 0, 0):
                        for i in range(4):
                            dve.wait_ge(sc_ready, q * 4 + (i + 1))
                            add_rows(i, acc_done)
                    if (kind, half) == ("up", 1) and c > 0:
                        low_t(c - 1)
                    if (kind, c, half) == ("gate", 1, 1):
                        gated(0)
                    if (kind, c, half) == ("down", 3, 1):
                        select(q + 1, q * PER + (base + 2))
                    if (kind, half) == ("down", 1) and c + 1 < EC:
                        gated(c + 1)
                    if (kind, c, half) == ("down", EC - 1, 0):
                        low_t(EC - 1)
                        split_gathered(q + 1)

            with dve.Fori(0, E) as q:
                expert(q)
            dve.wait_ge(place_done, 1)
            more = dve.value_load(full_i[0:1, 0:1])
            with dve.If(more > P):
                with dve.Fori(E, 2 * E) as q:
                    expert(q)
                dve.wait_ge(acc_done, 8 * E)
            dve.wait_ge(acc_done, 4 * E)
            for i in range(4):
                dve.wait_ge(sc_end, i + 1)
                add_rows(i, acc_end)
            dve.wait_ge(acc_end, 4)
            dve.wait_ge(gate_done, 8)
            gb = gate_f[:, :].rearrange("p (o d) -> p o d", o=1).to_broadcast([P, G, D])
            dve.tensor_tensor(acc[:, :, :], acc[:, :, :], gb, ALU.mult).then_inc(fin_acc, 1)
            dve.wait_ge(fin_acc, 1)
            dve.tensor_tensor(x[:, :, :], x[:, :, :], acc[:, :, :], ALU.add).then_inc(fin_x, 1)
            variance([(0, 2, D)])
            dve.wait_ge(rstd_done, 4 * L + 1)
            dve.wait_ge(final_in, 16)
            for g in range(G):
                dve.scalar_tensor_tensor(out=y[:, g, :], in0=x[:, g, :], scalar=rstd[:, g:g + 1], in1=final_gain[:, :],
                                         op0=ALU.mult, op1=ALU.mult).then_inc(fin_y, 1)

        @block.tensor
        def _(pe):
            mm = pe.matmul

            def product(o, lh, ll, rh, rl, first, last):
                mm(o, lh, rh, start=first, stop=False, skip_group_check=True)
                mm(o, lh, rl, start=False, stop=False, skip_group_check=True)
                return mm(o, ll, rh, start=False, stop=last, skip_group_check=True)

            plain = [0]

            def plain_unit():
                n = units_of["pe"][plain[0]]
                plain[0] += 1
                unit_wait(pe, n)
                return unit_view(n)

            def across(r, b, c0=None):
                pe.wait_ge(vec_used, 2 * r + 2)
                src = ring_sum[:, r % 2, :] if r < RINGED else ff_sum[:, r - RINGED, :]
                if c0 is None:
                    last = mm(bank[b][:, :], ones[:, :], src, start=True, stop=True)
                else:
                    for j in range(4):
                        last = mm(bank[b][:, c0 + j:c0 + j + 1], src[:, j * P:(j + 1) * P], ones[:, 0:1], start=True,
                                  stop=True, skip_group_check=True)
                last.then_inc(crossed, 1)

            s = [0]

            def split_unit():
                n = units_of["split"][s[0]]
                _, k, cols, _ = stream[n]
                sl = s[0] % SPLIT
                s[0] += 1
                pe.wait_ge(lo_done, s[0])
                f = lambda w: w[:, sl, 0:k * cols].rearrange("p (k n) -> p k n", k=k)
                return f(w_hi), f(w_lo)

            def transposes(m, ready):
                pe.wait_ge(y_done, ready)
                for j in range(4):
                    for a in range(2):
                        for g in range(G):
                            k = 2 * j + a
                            last = pe.transpose(bank[j][:, a * T + g * P:a * T + (g + 1) * P], y[:, g, k * P:(k + 1) * P],
                                                ident[:, :])
                    last.then_inc(h_tp, 1)

            def rows_product(banks, cols):
                for half in range(2):
                    wh, wl = split_unit()
                    for g in range(G):
                        for k in range(4):
                            kk = 4 * half + k
                            last = product(bank[banks + g][:, 0:cols], h_hi[:, kk, g * P:(g + 1) * P],
                                           h_lo[:, kk, g * P:(g + 1) * P], wh[:, k, :], wl[:, k, :], kk == 0, kk == 7)
                    last.then_inc(split_used, 1)

            def columns_half(b0, half):
                wh, wl = split_unit()
                for j in range(4):
                    for k in range(4):
                        kk = 4 * half + k
                        o = bank[b0 + j // 2][:, (j % 2) * T:(j % 2 + 1) * T]
                        js = slice(j * P, (j + 1) * P)
                        last = product(o, wh[:, k, js], wl[:, k, js], h_hi[:, kk, :], h_lo[:, kk, :],
                                       kk == 0 and j % 2 == 0, kk == 7)
                last.then_inc(split_used, 1)

            def columns_product(b0):
                columns_half(b0, 0)
                columns_half(b0, 1)

            pe.wait_ge(consts, 5)
            pe.wait_ge(c_silu, 1)
            pe.wait_ge(small_in, 16 * 8)
            pe.transpose(bank[0][:, 0:P], rows1[:, :], ident[:, :])
            pe.transpose(bank[0][:, P:P + 30], rows2[0:30, :], ident[0:30, 0:30]).then_inc(cols_tp, 1)
            pe.wait_ge(cols_done, 2)
            for r in range(4):
                across(r, 3, 4 * r)
            pe.wait_ge(mod_done, 2)
            ny = 0
            for l in range(L):
                m = ONE_LAYER * l
                ny += 2
                transposes(m, ny)
                pe.wait_ge(h_done, 8 * (m + 1))
                rows_product(0, LAT)
                rows_product(2, 512)
                columns_half(4, 0)
                if l == 0:
                    across(4, 6)
                pe.wait_ge(latn_done, 4 * (l + 1))
                pe.wait_ge(lat_done, 2 * (l + 1))
                for b in range(3):
                    for g in range(G):
                        o = bank[0][:, b * T + g * P:b * T + (g + 1) * P] if b < 2 else bank[1][:, g * P:(g + 1) * P]
                        last = pe.transpose(o, lat[:, g, b * P:(b + 1) * P], ident[:, :])
                    if b > 0:
                        last.then_inc(lat_tp, 1)
                columns_half(4, 1)
                uq = plain_unit()
                pe.wait_ge(latt_done, 3 * (l + 1))
                pe.wait_ge(vsb_done, 2 * (l + 1))
                for g in range(G):
                    bq = 2 if g == 0 else 0
                    for i, (a, w) in enumerate(((0, 5 * QW), (5 * QW, 3 * QW))):
                        for k in range(2):
                            last = mm(bank[bq + i][:, 0:w], lat_t[:, k, g * P:(g + 1) * P], uq[:, k, a:a + w],
                                      start=k == 0, stop=k == 1)
                last.then_inc(plain_used, 1)
                if l == 0:
                    across(5, 7)
                    pe.wait_ge(gate_done, 2)
                columns_half(6, 0)
                ukv = plain_unit()
                pe.wait_ge(qtok_done, 4 * (l + 1))
                for g in range(G):
                    bk = 2 if g == 0 else 0
                    for i in range(2):
                        last = mm(bank[bk + i][:, :], lat_t[:, 2, g * P:(g + 1) * P], ukv[:, 0, i * 512:(i + 1) * 512],
                                  start=True, stop=True)
                last.then_inc(plain_used, 1)
                columns_half(6, 1)
                for i in range(8):
                    src = q_tok if i < 4 else k_tok
                    if i == 0:
                        pe.wait_ge(qkrot_done, 6 * l + 4)
                        pe.wait_ge(qk_done, 4 * l + 2)
                    if i == 2:
                        pe.wait_ge(qk_done, 4 * l + 4)
                    if i == 4:
                        pe.wait_ge(qkrot_done, 6 * l + 6)
                        pe.wait_ge(vmla_done, 2 * (l + 1))
                        pe.wait_ge(kv_act, 4 * (l + 1))
                    for a in range(2):
                        for g in range(G):
                            last = pe.transpose(bank[(4 + i) % 8][0:QW, a * T + g * P:a * T + (g + 1) * P],
                                                src[:, g, 2 * (i % 4) + a, :], ident[:, :])
                    last.then_inc(qk_tp, 1)
                pe.wait_ge(qt_act, 4 * (l + 1))
                pe.wait_ge(qt_dve, 4 * (l + 1))
                if l == 0:
                    across(6, 7, 0)

                for i in range(6 + 3):
                    t = 6 * l + i
                    if i < 6:
                        if i >= 1:
                            pe.wait_ge(zm_done, t)
                        for a, h in enumerate(sb_heads(i)):
                            pp = slice((h % 2) * HD, (h % 2 + 1) * HD)
                            kb, qs, w = (1, slice(P, T), P) if i < 2 else (0, slice(0, T), T)
                            last = mm(bank[0][:, a * w:(a + 1) * w], k_sbt[pp, h // 2, kb * P:(kb + 1) * P],
                                      q_sbt[pp, h // 2, qs], start=(a == 0), stop=True, skip_group_check=True)
                        last.then_inc(z_ready, 1)
                        if i >= 1:
                            pe.wait_ge(max_done, t)
                        for a in range(4 if i < 2 else 2):
                            h = 4 * i + a if i < 2 else 2 * (i - 2) + a
                            g, w = (0, P) if i < 2 else (1, T)
                            last = mm(bank[4][:, a * w:(a + 1) * w], q_t[:, h, g * P:(g + 1) * P], k_t[:, h, 0:w],
                                      start=(a == 0), stop=True, skip_group_check=True)
                        last.then_inc(s_ready, 1)
                    if l == 0 and i == 3:
                        across(7, 7, 4)
                    if 1 <= i <= 6:
                        j = i - 1
                        t = 6 * l + j
                        pe.wait_ge(keep_done, t + 1)
                        if j >= 1:
                            pe.wait_ge(w_done, t)
                        kb = keep[:, j if j < 2 else 2 + j % 2, :]
                        last = mm(bank[1][:, :], from_here[:, :], kb, start=True, stop=j < 2, skip_group_check=True)
                        if j >= 2:
                            for a, h in enumerate(sb_heads(j)):
                                last = mm(bank[1][:, a * T + P:(a + 1) * T], ones[:, :],
                                          keep[:, h % 2, (h // 2) * P:(h // 2 + 1) * P], start=False, stop=a == 1,
                                          skip_group_check=True)
                        last.then_inc(cs_ready, 1)
                        pe.wait_ge(p_done, 16 * l + (4 * (j + 1) if j < 2 else 8 + 2 * (j - 1)))
                        if j >= 1:
                            pe.wait_ge(pt_done, t)
                        for a in range(4):
                            last = pe.transpose(bank[5][:, a * P:(a + 1) * P], probs[:, j % 2, a * P:(a + 1) * P],
                                                ident[:, :])
                        last.then_inc(p_tp, 1)
                    if 2 <= i <= 7:
                        j = i - 2
                        t = 6 * l + j
                        pe.wait_ge(pt_done, t + 1)
                        if l == 0 and j == 2:
                            pe.wait_ge(mod_done, 3)
                        for a in range(4):
                            if j < 2:
                                h, g, kb = 4 * j + a, 0, 0
                            else:
                                h, g, kb = 2 * (j - 2) + a // 2, 1, a % 2
                            last = mm(bank[6 + g][:, h * HD:(h + 1) * HD], probs_t[:, j % 2, a * P:(a + 1) * P],
                                      v_mla[:, kb, h * HD:(h + 1) * HD], start=(h == 0 and kb == 0), stop=(kb == g),
                                      skip_group_check=True)
                        last.then_inc(mpv_done, 1)
                    if i >= 3:
                        j = i - 3
                        t = 6 * l + j
                        pe.wait_ge(stick_done, t + 1)
                        for a, h in enumerate(sb_heads(j)):
                            if j < 2:
                                last = mm(bank[3][:, h * HD:(h + 1) * HD], sticks[:, j % 2, a * P:(a + 1) * P],
                                          v_sb[:, 1, h * HD:(h + 1) * HD], start=(j == 0 and a == 0), stop=False,
                                          skip_group_check=True)
                            else:
                                for g in range(G):
                                    last = mm(bank[2 + g][:, h * HD:(h + 1) * HD],
                                              sticks[:, j % 2, a * T + g * P:a * T + (g + 1) * P],
                                              v_sb[:, 0, h * HD:(h + 1) * HD], start=(j == 2 and a == 0 and g == 0),
                                              stop=True, skip_group_check=True)
                        last.then_inc(pv_done, 1)
                if l == 0:
                    across(8, 0, 0)
                    across(9, 0, 4)
                if l == 0:
                    pe.wait_ge(mod_done, 4)
                ny += 4
                transposes(m + 1, ny)
                pe.wait_ge(h_done, 8 * (m + 2))
                for c in range(2):
                    rows_product(4 + 2 * c, 512)
                ny += 2
                transposes(m + 2, ny)
                if l == 0:
                    pe.wait_ge(h_done, 8 * (m + 3))
                    for c in range(FC + 1):
                        if c < FC:
                            if c > 0:
                                pe.wait_ge(silu_done, 2 * c)
                            columns_product(0)
                            if c > 0:
                                pe.wait_ge(a_done, 2 * c)
                            columns_product(2)
                        if c > 0:
                            pe.wait_ge(a_done, 2 * c)
                            cc = c - 1
                            for pair in range(2):
                                wh, wl = split_unit()
                                for half in range(2):
                                    for g in range(G):
                                        for k in range(2):
                                            kk = 2 * pair + k
                                            cs = slice(half * 512, (half + 1) * 512)
                                            ts = slice(g * P, (g + 1) * P)
                                            last = product(bank[4 + 2 * half + g][:, :], a_hi[:, cc % 2, kk, ts],
                                                           a_lo[:, cc % 2, kk, ts], wh[:, k, cs], wl[:, k, cs],
                                                           cc == 0 and kk == 0, cc == FC - 1 and kk == 3)
                                last.then_inc(split_used, 1)
                        if c == FC - 1:
                            pe.wait_ge(silu_done, 2 * FC)
                            across(10, 0)
                            across(11, 1)
                    pe.wait_ge(a_done, 2 * FC)
                    for i in range(2):
                        for n in range(4):
                            across(12 + 4 * i + n, 2, 2 * KD * i + 4 * n)
                    across(20, 3)
                    pe.wait_ge(gate_done, 4)
                    across(21, 0)
                    across(22, 1)
                    pe.wait_ge(gate_done, 5)
                    across(23, 3)
                    pe.wait_ge(gate_done, 8)
                    pe.wait_ge(mod_done, 8)

            pe.wait_ge(router_in, 32)
            pe.wait_ge(hf_done, KD * L * ONE_LAYER)
            for g in range(G):
                for k in range(KD):
                    last = mm(bank[4][:, g * E:(g + 1) * E], hfm[:, k, g * P:(g + 1) * P], wr[:, k, :],
                              start=(g == 0 and k == 0), stop=k == KD - 1, skip_group_check=True)
            last.then_inc(lg_ready, 1)
            pe.wait_ge(ch_done, 2)
            o = lambda i: bank[5][:, i * E:(i + 1) * E]
            mm(o(0), before[:, :], chosen[:, 0, :], start=True, stop=True, skip_group_check=True)
            mm(o(1), before[:, :], chosen[:, 1, :], start=False, stop=False, skip_group_check=True)
            mm(o(1), ones[:, :], chosen[:, 0, :], start=False, stop=True, skip_group_check=True)
            mm(o(2), ones[:, :], chosen[:, 0, :], start=False, stop=False, skip_group_check=True)
            mm(o(2), ones[:, :], chosen[:, 1, :], start=False, stop=True, skip_group_check=True).then_inc(pos_ready, 1)

            def gather(q):
                pe.wait_ge(sel_done, q * 4 + 4)
                for k in range(KD):
                    for g in range(G):
                        last = mm(bank[6 + k // 4][:, (k % 4) * P:(k % 4 + 1) * P], y[:, g, k * P:(k + 1) * P], sel[:, g, :],
                                  start=(k % 4 == 0 and g == 0), stop=g == 1, skip_group_check=True)
                last.then_inc(hg_ready, 1)

            def weights_t(q):
                for g in range(G):
                    last = pe.transpose(bank[3][:, g * P:(g + 1) * P], sel_w[:, g, :], ident[:, :])
                last.then_inc(sw_tp, 1)

            def scatter(i, done):
                g, half = i // 2, i % 2
                mm(bank[6 + i % 2][:, :], sel_wt[:, g * P:(g + 1) * P], y_e[:, half * 512:(half + 1) * 512],
                   start=True, stop=True).then_inc(done, 1)

            gather(0)

            def expert(q):
                def unit(kind, c, half):
                    j = at[(kind, c, half)]
                    pe.wait_ge(lo_done, q * NU + (S0 + j + 1))
                    sl = (S0 + j) % SPLIT
                    k = 2 if kind == "down" else 4
                    f = lambda w: w[:, sl, :].rearrange("p (k n) -> p k n", k=k)
                    return f(w_hi), f(w_lo)

                def into(kind, c, b):
                    for half in range(2):
                        wh, wl = unit(kind, c, half)
                        for k in range(4):
                            kk = 4 * half + k
                            last = product(bank[b][:, :], hg_hi[:, kk, :], hg_lo[:, kk, :], wh[:, k, :], wl[:, k, :],
                                           kk == 0, kk == 7)
                        last.then_inc(split_used, 1)

                def act_t(c):
                    pe.wait_ge(ea_done, q * EC + (c + 1))
                    if c > 0:
                        pe.wait_ge(elo_done, q * EC + c)
                    for a in range(4):
                        last = pe.transpose(bank[2][:, a * P:(a + 1) * P], e_act[:, a * P:(a + 1) * P], ident[:, :])
                    last.then_inc(e_tp, 1)

                def down(c, pair):
                    pe.wait_ge(elo_done, q * EC + (c + 1))
                    wh, wl = unit("down", c, pair)
                    for half in range(2):
                        for k in range(2):
                            kk = 2 * pair + k
                            cs = slice(half * 512, (half + 1) * 512)
                            last = product(bank[4 + half][:, :], e_hi[:, c % 2, kk, :], e_lo[:, c % 2, kk, :],
                                           wh[:, k, cs], wl[:, k, cs], c == 0 and kk == 0, c == EC - 1 and kk == 3)
                    last.then_inc(split_used, 1)

                pe.wait_ge(hg_done, q * 4 + 4)
                for c in range(EC):
                    if c > 0:
                        pe.wait_ge(esilu, q * EC + c)
                    into("gate", c, 0)
                    if c == 0:
                        pe.wait_ge(ye_done, q * 2 + 2)
                        pe.wait_ge(sw_done, q + 1)
                        pe.wait_ge(hgf_done, q * KD + KD)
                        for i in range(4):
                            if i >= 2:
                                pe.wait_ge(acc_done, q * 4 + (i - 1))
                            scatter(i, sc_ready)
                        weights_t(q)
                    else:
                        act_t(c - 1)
                        pe.wait_ge(ea_done, q * EC + c)
                    into("up", c, 1)
                    if c > 0:
                        down(c - 1, 0)
                        if c == EC - 1:
                            act_t(EC - 1)
                        down(c - 1, 1)
                    if c == EC - 2:
                        pe.wait_ge(acc_done, q * 4 + 4)
                        gather(q + 1)
                down(EC - 1, 0)
                down(EC - 1, 1)

            with pe.Fori(0, E) as q:
                expert(q)
            pe.wait_ge(place_done, 1)
            more = pe.value_load(full_i[0:1, 0:1])
            with pe.If(more > P):
                with pe.Fori(E, 2 * E) as q:
                    expert(q)
                pe.wait_ge(sw_done, 2 * E + 1)
                pe.wait_ge(hgf_done, (2 * E + 1) * KD)
            pe.wait_ge(sw_done, E + 1)
            pe.wait_ge(hgf_done, (E + 1) * KD)
            pe.wait_ge(ye_end, 2)
            for i in range(4):
                if i >= 2:
                    pe.wait_ge(acc_end, i - 1)
                scatter(i, sc_end)


_INS = ["x", "c", "positions", "w_ada", "b_ada", "g_mix", "g_ffn", "w_in", "g_q_lat", "w_uq", "g_kv_lat", "w_ukv",
        "g_grp_mla", "g_grp_sb", "w_out", "w_ff_gate", "w_ff_up", "w_ff_down", "w_router", "b_router", "w_ex_gate",
        "w_ex_up", "w_ex_down", "g_final"]


def kernel(**inputs):
    import concourse.bacc as bacc
    from concourse.bass_utils import run_bass_kernel_spmd

    nc = bacc.Bacc("TRN2", target_bir_lowering=False, num_devices=1)
    arrays, args = {}, []
    for name in _INS:
        a = np.ascontiguousarray(inputs[name])
        arrays[f"in_{name}"] = a
        args.append(nc.dram_tensor(f"in_{name}", a.shape, mybir.dt.from_np(a.dtype), kind="ExternalInput").ap())
    shape = inputs["x"].shape
    out = nc.dram_tensor("out_trunk", shape, F32, kind="ExternalOutput").ap()
    trunk_kernel(nc, *args, out)
    r = run_bass_kernel_spmd(nc, [arrays], core_ids=[0])
    return r.results[0]["out_trunk"]
```

```python
from contextlib import ExitStack
from itertools import islice

import numpy as np

import concourse.bass as bass
from concourse import mybir

ALU = mybir.AluOpType
ACT = mybir.ActivationFunctionType
AX = mybir.AxisListType
F32 = mybir.dt.float32
F32R = mybir.dt.float32r
I32 = mybir.dt.int32
U32 = mybir.dt.uint32

P = 128
EPS = 1e-6
CHUNK = 64
MASKED = -1e30
ROPE_BASE = 10000.0
EXP_LN = "natural_log_exp_and_others"
ABSENT = 4096.0
RAW = 7
SPLIT = 3
UNIT = 2048

TURN = (6.28125, float(np.float32(0.0019350051879882812)), float(2 * np.pi - 6.28125 - 0.0019350051879882812))
ROUND = 12582912.0
PI_IN = 3.1415925


def trunk_kernel(nc, x_in, c_in, positions, w_ada, b_ada, g_mix, g_ffn, w_in, g_q_lat, w_uq, g_kv_lat,
                 w_ukv, g_grp_mla, g_grp_sb, w_out, w_ff_gate, w_ff_up, w_ff_down, w_router, b_router,
                 w_ex_gate, w_ex_up, w_ex_down, g_final, out):
    L, D, _ = w_ada.shape
    T = x_in.shape[1]
    G = T // P
    KD = D // P
    QL, KVL = g_q_lat.shape[1], g_kv_lat.shape[1]
    MW, SW = g_grp_mla.shape[1], g_grp_sb.shape[1]
    HD = 64
    H = SW // HD
    QW = w_uq.shape[2] // H
    RO = QW - HD
    RH = RO // 2
    LAT = QL + KVL + RO
    FF = w_ff_gate.shape[2]
    E, FE = w_ex_gate.shape[1], w_ex_gate.shape[3]
    FC, EC = FF // 512, FE // 512
    assert (L, G, KD, H, E) == (2, 2, 8, 8, 8) and MW == H * HD and KVL == P and QL == 2 * P

    stream = []
    ends = {}

    def end(name, use):
        ends[name] = sum(s[3] == use for s in stream)

    def k_rows(w, half, c0, n):
        return w[half * 512:(half + 1) * 512, c0:c0 + n].rearrange("(k p) n -> p k n", p=P)

    def add_ada(l, c, half):
        stream.append((k_rows(w_ada[l], half, c * 512, 512), 4, 512, "dve"))

    def add_cols(name, w, c0, n):
        for half in range(2):
            stream.append((k_rows(w, half, c0, n), 4, n, "split"))
        end(name, "split")

    def add_ff(kind, c, half):
        if kind == "down":
            r0 = c * 512 + half * 256
            stream.append((w_ff_down[0][r0:r0 + 256, :].rearrange("(k p) n -> p k n", p=P), 2, 1024, "split"))
        else:
            w = w_ff_gate if kind == "gate" else w_ff_up
            stream.append((k_rows(w[0], half, c * 512, 512), 4, 512, "split"))
        if half == 1:
            end((kind, c), "split")

    def ffn_order(chunks):
        o = []
        for c in range(chunks):
            o += [("gate", c, 0), ("gate", c, 1), ("up", c, 0), ("up", c, 1)]
            if c > 0:
                o += [("down", c - 1, 0), ("down", c - 1, 1)]
        return o + [("down", chunks - 1, 0), ("down", chunks - 1, 1)]

    order = ffn_order(EC)
    ff_order = ffn_order(FC)

    chunks = [(0, c) for c in range(12)] + [(1, c) for c in (0, 1, 2, 3, 6, 7, 8, 9, 4, 5, 10, 11)]
    IN_FF = range(10, 20)
    ada_units = [(l, c, half) for l, c in chunks for half in range(2)]
    FF_FIRST = 3
    ff_ada = {j: 1 for j in range(FF_FIRST, len(ff_order) - 1) if j % 4}
    ff_ada[FF_FIRST] = 2

    for u in ada_units[:8]:
        add_ada(*u)
    for l in range(L):
        ada = iter(ada_units[8:2 * IN_FF.start] if l == 0 else ada_units[2 * IN_FF.stop:])

        def add_next_ada(n):
            for u in islice(ada, n):
                add_ada(*u)

        def add_half(w, c0, n, half):
            stream.append((k_rows(w, half, c0, n), 4, n, "split"))

        add_cols(("lat", l), w_in[l], 0, LAT)
        add_cols(("v", l), w_in[l], LAT + 2 * SW, SW)
        add_next_ada(1)
        for half in range(2):
            add_half(w_in[l], LAT, SW, half)
            add_next_ada(1)
        end(("q", l), "split")
        stream.append((w_uq[l].rearrange("(k p) n -> p k n", p=P), 2, H * QW, "pe"))
        end(("uq", l), "pe")
        add_half(w_in[l], LAT + SW, SW, 0)
        add_next_ada(1)
        stream.append((w_ukv[l].rearrange("(k p) n -> p k n", p=P), 1, 2 * MW, "pe"))
        end(("ukv", l), "pe")
        add_half(w_in[l], LAT + SW, SW, 1)
        end(("k", l), "split")
        add_next_ada(1 if l == 0 else 0)
        for c in range(2):
            for half in range(2):
                add_half(w_out[l], c * 512, 512, half)
                if (c, half) == (0, 0) and l == 0:
                    add_next_ada(1)
                if (c, half) == (1, 0):
                    add_next_ada(4 if l == 0 else 2)
            end(("out", l, c), "split")
        add_next_ada(2)
        if l == 0:
            n_ff = len(stream)
            done = 2 * IN_FF.start
            for j, u in enumerate(ff_order):
                add_ff(*u)
                for _ in range(ff_ada.get(j, 0)):
                    add_ada(*ada_units[done])
                    done += 1
            assert done == 2 * IN_FF.stop
            n_second = len(stream)
    N0 = len(stream)
    split_at = {}
    counts = {"split": 0, "pe": 0, "dve": 0}
    for n, s in enumerate(stream):
        split_at[n] = counts[s[3]]
        counts[s[3]] += 1
    units_of = {use: [n for n, s in enumerate(stream) if s[3] == use] for use in counts}
    S0 = counts["split"]
    NU = len(order)
    at = {u: j for j, u in enumerate(order)}

    def sb_heads(i):
        return [i, i + 2, i + 4, i + 6] if i < 2 else [4 * ((i - 2) // 2) + (i - 2) % 2 + a for a in (0, 2)]

    assert NU % RAW == 0 and NU % SPLIT == 0

    with ExitStack() as ctx:
        def sb(name, shape, dt=F32, where=None):
            return (where or ctx).enter_context(nc.sbuf_tensor(name, shape, dt))

        def sem(name):
            return ctx.enter_context(nc.semaphore(name))

        bank = [ctx.enter_context(nc.psum_tensor(f"bank{i}", [P, 512], F32)) for i in range(8)]

        raw = sb("raw", [P, RAW, UNIT])
        w_hi = sb("w_hi", [P, SPLIT, UNIT], F32R)
        w_lo = sb("w_lo", [P, SPLIT, UNIT], F32R)
        x = sb("x", [P, G, D])
        y = sb("y", [P, G, D])
        gate_m = sb("gate_m", [P, D])
        gate_f = sb("gate_f", [P, D])
        early = ExitStack()
        q_t = sb("q_t", [QW, H, T], where=early)
        k_t = sb("k_t", [QW, H, T], where=early)
        early.close()
        h_hi = sb("h_hi", [P, KD, T], F32R)
        h_lo = sb("h_lo", [P, KD, T], F32R)
        ident = sb("ident", [P, P])
        ones = sb("ones", [P, P])
        from_here = sb("from_here", [P, P])
        before = sb("before", [P, P])
        strict = sb("strict", [P, T])
        chunked = sb("chunked", [P, T])
        slot_no = sb("slot_no", [P, P])
        cols1 = sb("cols1", [P, P])
        cols2 = sb("cols2", [P, 32])
        mod = sb("mod", [P, L, 2, 2, KD])
        modt = sb("modt", [P, 2, KD])
        squares = sb("squares", [P, 4])
        rstd = sb("rstd", [P, 4])
        cos2 = sb("cos2", [P, G, 1, RO])
        sin2 = sb("sin2", [P, G, 1, RO])
        ring_sum = sb("ring_sum", [P, 2, 512])

        final_gain = sb("final_gain", [P, D])
        wr = sb("wr", [P, KD, E])
        br = sb("br", [P, E])

        over = ExitStack()
        lat = sb("lat", [P, G, LAT], where=over)
        lat_t = sb("lat_t", [P, 3, T], where=over)
        v_sb = sb("v_sb", [P, G, SW], where=over)
        q_sbt = sb("q_sbt", [P, 4, T], where=over)
        k_sbt = sb("k_sbt", [P, 4, T], where=over)
        v_mla = sb("v_mla", [P, G, MW], where=over)
        probs = sb("probs", [P, 2, 512], where=over)
        probs_t = sb("probs_t", [P, 2, 512], where=over)
        neg_max = sb("neg_max", [P, 2 * H], where=over)
        sums = sb("sums", [P, 2 * H], where=over)
        recip = sb("recip", [P, 2 * H], where=over)
        rot = sb("rot", [P, 2, G, H, RO], where=over)
        rot_a, rot_b = rot[:, 0], rot[:, 1]
        sticks = rot[:, :, :, :, :].rearrange("p i g h c -> p i (g h c)")
        here = ExitStack()
        q_tok = sb("q_tok", [P, G, H, QW], where=here)
        k_tok = sb("k_tok", [P, G, H, QW], where=here)
        here.close()
        sub = ExitStack()
        zm = sb("zm", [P, 3, 512], where=sub)
        keep = sb("keep", [P, 4, 512], where=sub)
        sub.close()
        hf = sb("hf", [P, KD, T], where=over)
        over.close()
        ffn = ExitStack()
        act = sb("act", [P, 4, T], where=ffn)
        a_hi = sb("a_hi", [P, 2, 4, T], F32R, where=ffn)
        a_lo = sb("a_lo", [P, 2, 4, T], F32R, where=ffn)
        norm_only = ExitStack()
        hfn = sb("hfn", [P, KD, T], where=norm_only)
        norm_only.close()
        ff_sum = sb("ff_sum", [P, len(IN_FF), 512], where=ffn)
        ffn.close()
        moe = ExitStack()
        hfm = sb("hfm", [P, KD, T], where=moe)
        e_act = sb("e_act", [P, 512], where=moe)
        e_hi = sb("e_hi", [P, 2, 4, P], F32R, where=moe)
        e_lo = sb("e_lo", [P, 2, 4, P], F32R, where=moe)
        hgf = sb("hgf", [P, KD, P], where=moe)
        hg_hi = sb("hg_hi", [P, KD, P], F32R, where=moe)
        hg_lo = sb("hg_lo", [P, KD, P], F32R, where=moe)
        ye_hi = sb("ye_hi", [P, D], F32R, where=moe)
        ye_lo = sb("ye_lo", [P, D], F32R, where=moe)
        acc = sb("acc", [P, G, D], where=moe)
        sel = sb("sel", [P, G, P], where=moe)
        sel_t = sb("sel_t", [P, T], F32R, where=moe)
        logits = sb("logits", [P, G, E], where=moe)
        logits_t = e_act[0:E, 0:T]
        top = sb("top", [P, G, 8], where=moe)
        topi = sb("topi", [P, G, 8], U32, where=moe)
        topf = sb("topf", [P, G, 8], where=moe)
        hot = sb("hot", [P, G, 2, E], where=moe)
        tw = sb("tw", [P, G, 4], where=moe)
        chosen = sb("chosen", [P, G, E], where=moe)
        comb = sb("comb", [P, G, E], where=moe)
        place = sb("place", [P, 2 * E + 1, 4], where=moe)
        now = sb("now", [P, 4], where=moe)
        w_before = sb("w_before", [P, G], where=moe)
        full = sb("full", [P, 1], where=moe)
        full_i = sb("full_i", [P, 1], I32, where=moe)
        moe.close()
        pre = ExitStack()
        rows1 = sb("rows1", [P, P], where=pre)
        rows2 = sb("rows2", [P, P], where=pre)
        pos_i = sb("pos_i", [P, G], I32, where=pre)
        pos_f = sb("pos_f", [P, G], where=pre)
        freq = sb("freq", [P, RH], where=pre)
        ang = sb("ang", [P, G, RH], where=pre)
        turns = sb("turns", [P, 2, G, RH], where=pre)
        rest = sb("rest", [P, 2, G, RH], where=pre)
        trig = sb("trig", [P, 2, G, RH], where=pre)
        pre.close()

        unit_in = [sem(f"unit_in{i}") for i in range(RAW)]
        small_in = sem("small_in"); pos_in = sem("pos_in"); x_in_s = sem("x_in_s")
        bias_in = sem("bias_in"); router_in = sem("router_in"); final_in = sem("final_in")
        hi_done = sem("hi_done"); lo_done = sem("lo_done")
        split_used = sem("split_used"); plain_used = sem("plain_used")
        consts = sem("consts"); c_silu = sem("c_silu"); cols_tp = sem("cols_tp"); cols_done = sem("cols_done")
        angles = sem("angles"); trig_done = sem("trig_done"); trig2 = sem("trig2")
        vec_used = sem("vec_used"); crossed = sem("crossed"); mod_done = sem("mod_done"); gate_done = sem("gate_done")
        sq_done = sem("sq_done"); var_done = sem("var_done"); rstd_done = sem("rstd_done"); y_done = sem("y_done")
        h_tp = sem("h_tp"); hf_done = sem("hf_done"); h_done = sem("h_done")
        lat_done = sem("lat_done"); vsb_done = sem("vsb_done"); qk_done = sem("qk_done")
        z_ready = sem("z_ready"); zm_done = sem("zm_done"); ln_done = sem("ln_done"); keep_done = sem("keep_done")
        cs_ready = sem("cs_ready"); w_done = sem("w_done"); stick_done = sem("stick_done"); pv_done = sem("pv_done")
        osb_done = sem("osb_done")
        latn_done = sem("latn_done"); lat_tp = sem("lat_tp"); latt_done = sem("latt_done")
        kv_act = sem("kv_act"); qtok_done = sem("qtok_done"); vmla_done = sem("vmla_done"); qkrot_done = sem("qkrot_done")
        qk_tp = sem("qk_tp"); qt_act = sem("qt_act"); qt_dve = sem("qt_dve")
        s_ready = sem("s_ready"); max_done = sem("max_done"); p_done = sem("p_done"); p_tp = sem("p_tp")
        pt_done = sem("pt_done"); mpv_done = sem("mpv_done"); omla_done = sem("omla_done")
        quarter_done = sem("quarter_done"); x_done = sem("x_done")
        silu_done = sem("silu_done"); a_done = sem("a_done")
        lgt_ready = sem("lgt_ready"); lgt_done = sem("lgt_done"); lg_ready = sem("lg_ready")
        rd_done = sem("rd_done"); re_done = sem("re_done"); ch_done = sem("ch_done"); pos_ready = sem("pos_ready")
        place_done = sem("place_done")
        sel_done = sem("sel_done"); hg_ready = sem("hg_ready"); hgf_done = sem("hgf_done"); hg_done = sem("hg_done")
        sw_tp = sem("sw_tp"); sw_done = sem("sw_done")
        esilu = sem("esilu"); ea_done = sem("ea_done")
        e_tp = sem("e_tp"); ehi_done = sem("ehi_done"); elo_done = sem("elo_done")
        ye_done = sem("ye_done"); yl_done = sem("yl_done"); sc_ready = sem("sc_ready"); acc_done = sem("acc_done")
        acc_zero = sem("acc_zero"); ye_end = sem("ye_end"); yl_end = sem("yl_end"); sc_end = sem("sc_end")
        acc_end = sem("acc_end"); fin_acc = sem("fin_acc"); fin_x = sem("fin_x"); fin_y = sem("fin_y")
        out_done = sem("out_done")
        act_own = sem("act_own"); dve_own = sem("dve_own"); pool_own = sem("pool_own")

        ONE_LAYER = 3
        block = ctx.enter_context(nc.Block())

        def unit_view(n):
            _, k, cols, _ = stream[n]
            return raw[:, n % RAW, 0:k * cols].rearrange("p (k n) -> p k n", k=k)

        def unit_wait(eng, n):
            eng.wait_ge(unit_in[n % RAW], 16 * (n // RAW + 1))

        @block.sync
        def _(sp):
            def load(n):
                if n >= RAW:
                    old = n - RAW
                    sp.wait_ge({"split": lo_done, "pe": plain_used, "dve": vec_used}[stream[old][3]], split_at[old] + 1)
                sp.dma_start(unit_view(n), stream[n][0]).then_inc(unit_in[n % RAW], 16)

            r1 = b_ada.rearrange("l (r p) -> (l r) p", p=P)
            nb = L * 6 * KD
            sp.dma_start(rows2[0:8, :], c_in.rearrange("b (r p) -> (b r) p", p=P)).then_inc(small_in, 16)
            sp.dma_start(rows2[8:12, :], g_q_lat.rearrange("l (r p) -> (l r) p", p=P)).then_inc(small_in, 16)
            sp.dma_start(rows2[12:14, :], g_kv_lat).then_inc(small_in, 16)
            sp.dma_start(rows2[14:22, :], g_grp_mla.rearrange("l (r p) -> (l r) p", p=P)).then_inc(small_in, 16)
            sp.dma_start(rows2[22:30, :], g_grp_sb.rearrange("l (r p) -> (l r) p", p=P)).then_inc(small_in, 16)
            sp.dma_start(rows1[0:nb, :], r1).then_inc(small_in, 16)
            sp.dma_start(rows1[nb:nb + 16, :], g_mix.rearrange("l (r p) -> (l r) p", p=P)).then_inc(small_in, 16)
            sp.dma_start(rows1[nb + 16:nb + 32, :], g_ffn.rearrange("l (r p) -> (l r) p", p=P)).then_inc(small_in, 16)
            for n in range(2):
                load(n)
            sp.dma_start(x[:, :, :], x_in[0].rearrange("(g p) d -> p g d", p=P)).then_inc(x_in_s, 16)
            with nc.allow_non_contiguous_dma(reason="256 positions, one to a partition"):
                sp.dma_start(pos_i[:, :], positions[0].rearrange("(g p) -> p g", p=P)).then_inc(pos_in, 16)
            bias = lambda l, part: b_ada[l:l + 1, part * D:(part + 1) * D].to_broadcast([P, D])
            for n in range(2, N0):
                if n == 10:
                    for part, t in ((2, gate_m), (5, gate_f)):
                        sp.dma_start(t[:, :], bias(0, part)).then_inc(bias_in, 16)
                if n == n_ff + 8:
                    sp.wait_ge(x_done, 4)
                    sp.dma_start(gate_m[:, :], bias(1, 2)).then_inc(bias_in, 16)
                if n == n_second + RAW + 1:
                    sp.wait_ge(x_done, 8)
                    sp.dma_start(gate_f[:, :], bias(1, 5)).then_inc(bias_in, 16)
                load(n)
            def load_expert(q, e):
                for j, (kind, c, half) in enumerate(order):
                    slot = (N0 + j) % RAW
                    sp.wait_ge(lo_done, q * NU + (S0 + j - RAW + 1))
                    if kind == "down":
                        r0 = c * 512 + half * 256
                        src = w_ex_down[0, bass.ds(e, 1), r0:r0 + 256, :].rearrange("o (k p) n -> p (o k) n", p=P)
                        dst = raw[:, slot, :].rearrange("p (k n) -> p k n", k=2)
                    else:
                        w = w_ex_gate if kind == "gate" else w_ex_up
                        src = w[0, bass.ds(e, 1), half * 512:(half + 1) * 512, c * 512:(c + 1) * 512].rearrange(
                            "o (k p) n -> p (o k) n", p=P)
                        dst = raw[:, slot, :].rearrange("p (k n) -> p k n", k=4)
                    sp.dma_start(dst, src).then_inc(unit_in[slot], 16)

            sp.dma_start(final_gain[:, :], g_final.rearrange("(o d) -> o d", o=1).to_broadcast([P, D])).then_inc(final_in, 16)
            sp.dma_start(wr[:, :, :], w_router[0].rearrange("(k p) e -> p k e", p=P)).then_inc(router_in, 16)
            sp.dma_start(br[:, :], b_router[0:1, :].to_broadcast([P, E])).then_inc(router_in, 16)
            sp.wait_ge(plain_used, counts["pe"])
            sp.wait_ge(vec_used, counts["dve"])
            sp.wait_ge(lo_done, S0)
            with sp.Fori(0, E) as q:
                load_expert(q, q)
            sp.wait_ge(place_done, 1)
            more = sp.value_load(full_i[0:1, 0:1])
            with sp.If(more > P):
                with sp.Fori(0, E) as e:
                    load_expert(e + E, e)
            for g in range(G):
                sp.wait_ge(fin_y, g + 1)
                sp.dma_start(out[0, g * P:(g + 1) * P, :], y[:, g, :]).then_inc(out_done, 16)
            sp.wait_ge(out_done, 16 * G)

        @block.gpsimd
        def _(pool):
            n = 0
            for t in (ident, from_here, before, chunked, strict, ones, slot_no):
                if t is slot_no:
                    pool.iota(t[:, :], pattern=[[1, P]], base=0, channel_multiplier=0,
                              allow_small_or_imprecise_dtypes=True).then_inc(pool_own, 1)
                else:
                    pool.memset(t[:, :], 1.0 if t in (ones, from_here, before) else 0.0).then_inc(pool_own, 1)
                n += 1
            for i in range(RH):
                f = float(np.float32(np.power(np.float32(ROPE_BASE), np.float32(-i / RH))))
                pool.memset(freq[:, i:i + 1], f).then_inc(pool_own, 1)
                n += 1
            pool.wait_ge(pool_own, n)
            pool.affine_select(out=ident[:, :], in_=ident[:, :], compare_op=ALU.not_equal, fill=1.0, base=0,
                               pattern=[[-1, P]], channel_multiplier=1).then_inc(consts, 1)
            pool.affine_select(out=from_here[:, :], in_=from_here[:, :], compare_op=ALU.is_ge, fill=0.0, base=0,
                               pattern=[[-1, P]], channel_multiplier=1).then_inc(consts, 1)
            pool.affine_select(out=before[:, :], in_=before[:, :], compare_op=ALU.is_gt, fill=0.0, base=0,
                               pattern=[[1, P]], channel_multiplier=-1).then_inc(consts, 1)
            pool.affine_select(out=strict[:, 0:P], in_=strict[:, 0:P], compare_op=ALU.is_gt, fill=MASKED, base=0,
                               pattern=[[1, P]], channel_multiplier=-1).then_inc(consts, 1)
            pool.memset(chunked[0:CHUNK, P + CHUNK:2 * P], MASKED).then_inc(consts, 1)
            pool.wait_ge(x_done, 8 * L - 4)
            pool.memset(acc[:, :, :], 0.0).then_inc(acc_zero, 1)

        @block.scalar
        def _(act_e):
            own = [0]

            def link(ins):
                ins.then_inc(act_own, 1)
                own[0] += 1
                act_e.wait_ge(act_own, own[0])

            def hi(s):
                n = units_of["split"][s]
                words = stream[n][1] * stream[n][2]
                unit_wait(act_e, n)
                if s >= SPLIT:
                    act_e.wait_ge(split_used, s - SPLIT + 1)
                act_e.activation(w_hi[:, s % SPLIT, 0:words], raw[:, n % RAW, 0:words], ACT.Copy).then_inc(hi_done, 1)

            def rstd_of(m, n):
                act_e.wait_ge(var_done, m + 1)
                link(act_e.activation(rstd[:, 0:n], squares[:, 0:n], ACT.Ln))
                act_e.activation(rstd[:, 0:n], rstd[:, 0:n], ACT.Exp, scale=-0.5).then_inc(rstd_done, 1)

            def evacuate(m, dst, gain, shift):
                for k in range(KD):
                    if k % 2 == 0:
                        act_e.wait_ge(h_tp, 4 * m + k // 2 + 1)
                    src = bank[k // 2][:, (k % 2) * T:(k % 2 + 1) * T]
                    if shift is None:
                        act_e.activation(dst[:, k, :], src, ACT.Copy, scale=gain(k)).then_inc(hf_done, 1)
                    else:
                        act_e.activation(dst[:, k, :], src, ACT.Identity, bias=shift(k), scale=gain(k)).then_inc(hf_done, 1)

            act_e.wait_ge(small_in, 16 * 8)
            act_e.activation(rows2[0:8, :], rows2[0:8, :], ACT.Silu).then_inc(c_silu, 1)
            s = 0
            for l in range(L):
                act_e.preload_act_table_set(EXP_LN)
                m = ONE_LAYER * l
                gcol = lambda i: (lambda k, i=i: mod[:, l, i, 1, k:k + 1])
                scol = lambda i: (lambda k, i=i: mod[:, l, i, 0, k:k + 1])
                if l == 0:
                    act_e.wait_ge(x_in_s, 16)
                else:
                    hi(s); s += 1
                    hi(s); s += 1
                for g in range(G):
                    if l > 0:
                        act_e.wait_ge(x_done, 8 * l - 1 + g)
                    act_e.activation(y[:, g, :], x[:, g, :], ACT.Square, accum_out=squares[:, g:g + 1]).then_inc(sq_done, 1)
                rstd_of(4 * l, G)
                if l == 0:
                    hi(s); s += 1
                act_e.wait_ge(mod_done, 4 * l + 2)
                evacuate(m, hf, gcol(0), scol(0))
                for _ in range(3 if l == 0 else 2):
                    hi(s); s += 1
                if l == 0:
                    act_e.wait_ge(angles, 1)
                    act_e.activation(trig[:, :, :, :], rest[:, :, :, :], ACT.Sin).then_inc(trig_done, 1)
                    act_e.preload_act_table_set(EXP_LN)
                hi(s); s += 1
                if l == 0:
                    act_e.wait_ge(trig2, 4)

                def out_of_psum(i):
                    act_e.wait_ge(split_used, ends["q" if i < 2 else "k", l])
                    dst = (q_sbt if i < 2 else k_sbt)[:, 2 * (i % 2):2 * (i % 2) + 2, :]
                    act_e.activation(dst, bank[4 + i][:, :].rearrange("p (a t) -> p a t", t=T), ACT.Copy,
                                     scale=HD ** -0.5 if i < 2 else 1.0).then_inc(qk_done, 1)

                act_e.wait_ge(split_used, ends["lat", l])
                for g in range(G):
                    act_e.activation(lat[:, g, :], bank[g][:, 0:LAT], ACT.Copy).then_inc(lat_done, 1)
                act_e.wait_ge(lat_done, 2 * (l + 1))
                for g in range(G):
                    act_e.activation(y[:, g, 0:QL], lat[:, g, 0:QL], ACT.Square,
                                     accum_out=squares[:, g:g + 1]).then_inc(sq_done, 1)
                    act_e.activation(y[:, g, QL:QL + KVL], lat[:, g, QL:QL + KVL], ACT.Square,
                                     accum_out=squares[:, 2 + g:3 + g]).then_inc(sq_done, 1)
                hi(s); s += 1
                rstd_of(4 * l + 1, 4)
                act_e.wait_ge(split_used, ends["v", l])
                for g in range(G):
                    act_e.activation(v_sb[:, g, :], bank[2 + g][:, :], ACT.Copy).then_inc(vsb_done, 1)
                hi(s); s += 1
                hi(s); s += 1
                act_e.wait_ge(lat_tp, 2 * l + 2)
                for b in range(3):
                    col = 8 + 2 * l + b if b < 2 else 12 + l
                    src = bank[0][:, b * T:(b + 1) * T] if b < 2 else bank[1][:, 0:T]
                    act_e.activation(lat_t[:, b, :], src, ACT.Copy, scale=cols2[:, col:col + 1]).then_inc(latt_done, 1)
                out_of_psum(0)
                out_of_psum(1)
                act_e.wait_ge(plain_used, ends["uq", l])
                for g in range(G):
                    bq = 2 if g == 0 else 0
                    act_e.activation(q_tok[:, g, 0:5, :], bank[bq][:, 0:5 * QW].rearrange("p (h c) -> p h c", c=QW),
                                     ACT.Copy, scale=float(QW) ** -0.5).then_inc(qtok_done, 1)
                    act_e.activation(q_tok[:, g, 5:8, :], bank[bq + 1][:, 0:3 * QW].rearrange("p (h c) -> p h c", c=QW),
                                     ACT.Copy, scale=float(QW) ** -0.5).then_inc(qtok_done, 1)
                hi(s); s += 1
                act_e.wait_ge(plain_used, ends["ukv", l])
                for i in range(2):
                    kv = bank[2 + i][:, :].rearrange("p (h c) -> p h c", c=P)
                    act_e.activation(k_tok[:, 0, 4 * i:4 * i + 4, 0:HD], kv[:, :, 0:HD], ACT.Copy).then_inc(kv_act, 1)
                    act_e.activation(v_mla[:, 0, i * 256:(i + 1) * 256].rearrange("p (h c) -> p h c", c=HD),
                                     kv[:, :, HD:P], ACT.Copy).then_inc(kv_act, 1)
                hi(s); s += 1
                out_of_psum(2)
                out_of_psum(3)
                for i in range(0, 8, 2):
                    act_e.wait_ge(qk_tp, 8 * l + i + 1)
                    dst = (q_t if i < 4 else k_t)[:, 2 * (i % 4):2 * (i % 4) + 2, :]
                    act_e.activation(dst, bank[(4 + i) % 8][0:QW, :].rearrange("p (h t) -> p h t", t=T),
                                     ACT.Copy).then_inc(qt_act, 1)
                hi(s); s += 1

                for i in range(6 + 2):
                    if i < 6:
                        t = 6 * l + i
                        kb = keep[:, i if i < 2 else 2 + i % 2, :]
                        act_e.wait_ge(zm_done, t + 1)
                        if i >= 4:
                            act_e.wait_ge(cs_ready, t - 1)
                        link(act_e.activation(kb, zm[:, i % 3, :], ACT.Abs))
                        link(act_e.activation(kb, kb, ACT.Exp, scale=-1.0))
                        act_e.activation(kb, kb, ACT.Ln, bias=1.0).then_inc(ln_done, 1)
                        act_e.wait_ge(max_done, t + 1)
                        heads = 4 if i < 2 else 2
                        w = 512 // heads
                        c0 = 4 * i if i < 2 else H + 2 * (i - 2)
                        for h in range(heads):
                            pr = probs[:, i % 2, h * w:(h + 1) * w]
                            act_e.activation(pr, pr, ACT.Exp, bias=neg_max[:, c0 + h:c0 + h + 1],
                                             accum_out=sums[:, c0 + h:c0 + h + 1]).then_inc(p_done, 1)
                    if i >= 2:
                        j = i - 2
                        t = 6 * l + j
                        act_e.wait_ge(w_done, t + 1)
                        if j >= 2:
                            act_e.wait_ge(pv_done, t - 1)
                        act_e.activation(sticks[:, j % 2, :], zm[:, j % 3, :], ACT.Exp).then_inc(stick_done, 1)
                act_e.wait_ge(stick_done, 6 * (l + 1))
                for i in range(2):
                    act_e.wait_ge(omla_done if i == 0 else osb_done, 2 * (l + 1))
                    for g in range(G):
                        act_e.activation(hf[:, 4 * g + 2 * i:4 * g + 2 * i + 2, :], y[:, g, i * 512:(i + 1) * 512].rearrange("p (a b) -> p a b", a=2),
                                         ACT.Square, accum_out=squares[:, 2 * g + i:2 * g + i + 1]).then_inc(sq_done, 1)
                rstd_of(4 * l + 2, 4)
                evacuate(m + 1, hf, lambda k: cols2[:, (14 + 4 * l + k if k < 4 else 22 + 4 * l + k - 4):][:, 0:1], None)
                hi(s); s += 1
                if l == 0:
                    for _ in range(3):
                        hi(s); s += 1
                for g in range(G):
                    act_e.wait_ge(x_done, 8 * l + 3 + g)
                    act_e.activation(y[:, g, :], x[:, g, :], ACT.Square, accum_out=squares[:, g:g + 1]).then_inc(sq_done, 1)
                rstd_of(4 * l + 3, G)
                act_e.wait_ge(mod_done, 4 * l + 4)
                evacuate(m + 2, hfn if l == 0 else hfm, gcol(1), scol(1))
                if l == 0:
                    for j, (kind, c, half) in enumerate(ff_order):
                        if j >= FF_FIRST:
                            hi(s); s += 1
                        if (kind, half) == ("up", 1):
                            act_e.wait_ge(split_used, ends["gate", c])
                            if c > 0:
                                act_e.wait_ge(a_done, 2 * c)
                            for i in range(2):
                                act_e.activation(act[:, 2 * i:2 * i + 2, :], bank[i][:, :].rearrange("p (k t) -> p k t", t=T),
                                                 ACT.Silu).then_inc(silu_done, 1)

            act_e.wait_ge(rd_done, 1)
            act_e.activation(tw[:, :, 1], tw[:, :, 0], ACT.Exp).then_inc(re_done, 1)

            def evacuate_rows(done):
                for i in range(2):
                    act_e.activation(ye_hi[:, i * 512:(i + 1) * 512], bank[4 + i][:, :], ACT.Copy).then_inc(done, 1)

            def evacuate_gathered(q, half):
                act_e.wait_ge(hg_ready, q * 2 + (half + 1))
                for k in range(4 * half, 4 * half + 4):
                    act_e.activation(hgf[:, k, :], bank[6 + k // 4][:, (k % 4) * P:(k % 4 + 1) * P], ACT.Identity,
                                     bias=mod[:, 1, 1, 0, k:k + 1], scale=mod[:, 1, 1, 1, k:k + 1]).then_inc(hgf_done, 1)

            def evacuate_selection(q):
                act_e.wait_ge(sw_tp, q + 1)
                act_e.activation(sel_t[:, :], bank[3][:, 0:T], ACT.Copy).then_inc(sw_done, 1)

            def expert(q):
                def hi_e(j):
                    act_e.wait_ge(unit_in[(N0 + j) % RAW], q * (16 * NU // RAW) + 16 * ((N0 + j) // RAW + 1))
                    act_e.wait_ge(split_used, q * NU + (S0 + j - SPLIT + 1))
                    act_e.activation(w_hi[:, (S0 + j) % SPLIT, :], raw[:, (N0 + j) % RAW, :], ACT.Copy).then_inc(hi_done, 1)

                def silu(c):
                    act_e.wait_ge(split_used, q * NU + (S0 + at["gate", c, 1] + 1))
                    act_e.activation(e_act[:, :], bank[0][:, :], ACT.Silu).then_inc(esilu, 1)

                def high_t(c):
                    act_e.wait_ge(e_tp, q * EC + (c + 1))
                    act_e.activation(e_hi[:, c % 2, :, :], bank[2][:, :].rearrange("p (k t) -> p k t", t=P),
                                     ACT.Copy).then_inc(ehi_done, 1)

                for j, (kind, c, half) in enumerate(order):
                    hi_e(j)
                    if (kind, c, half) == ("gate", 0, 1):
                        act_e.wait_ge(split_used, q * NU + S0)
                        evacuate_rows(ye_done)
                    if (kind, half) == ("up", 1):
                        if c > 0:
                            high_t(c - 1)
                        silu(c)
                    if (kind, c, half) == ("gate", 0, 0):
                        evacuate_gathered(q, 0)
                        evacuate_gathered(q, 1)
                    if (kind, c, half) == ("gate", 1, 0):
                        evacuate_selection(q)
                    if (kind, c, half) == ("down", EC - 1, 0):
                        high_t(EC - 1)

            act_e.preload_act_table(ACT.Silu)
            with act_e.Fori(0, E) as q:
                expert(q)
            act_e.wait_ge(place_done, 1)
            more = act_e.value_load(full_i[0:1, 0:1])
            with act_e.If(more > P):
                with act_e.Fori(E, 2 * E) as q:
                    expert(q)
                act_e.wait_ge(split_used, S0 + 2 * E * NU)
            act_e.wait_ge(split_used, S0 + E * NU)
            evacuate_rows(ye_end)
            act_e.preload_act_table_set(EXP_LN)
            for g in range(G):
                act_e.wait_ge(fin_x, 2 * g + 2)
                act_e.activation(y[:, g, :], x[:, g, :], ACT.Square, accum_out=squares[:, g:g + 1]).then_inc(sq_done, 1)
            rstd_of(4 * L, G)

        @block.vector
        def _(dve):
            own = [0]

            def link(ins):
                ins.then_inc(dve_own, 1)
                own[0] += 1
                dve.wait_ge(dve_own, own[0])

            def lo(s):
                n = units_of["split"][s]
                words = stream[n][1] * stream[n][2]
                dve.wait_ge(hi_done, s + 1)
                dve.tensor_tensor(w_lo[:, s % SPLIT, 0:words], raw[:, n % RAW, 0:words],
                                  w_hi[:, s % SPLIT, 0:words].bitcast(F32), ALU.subtract).then_inc(lo_done, 1)

            nsq = [0]

            def variance(cols):
                nsq[0] += cols[-1][1]
                dve.wait_ge(sq_done, nsq[0])
                for i, (a, b, w) in enumerate(cols):
                    ins = dve.tensor_scalar(squares[:, a:b], squares[:, a:b], 1.0 / w, EPS, ALU.mult, ALU.add)
                    if i + 1 < len(cols):
                        link(ins)
                ins.then_inc(var_done, 1)

            def split_operand(m, src):
                for j in range(4):
                    dve.wait_ge(hf_done, 8 * m + 2 * j + 2)
                    part = slice(2 * j, 2 * j + 2)
                    dve.tensor_copy(h_hi[:, part, :], src[:, part, :]).then_inc(h_done, 1)
                    dve.wait_ge(h_done, 8 * m + 2 * j + 1)
                    dve.tensor_tensor(h_lo[:, part, :], src[:, part, :], h_hi[:, part, :].bitcast(F32),
                                      ALU.subtract).then_inc(h_done, 1)

            def normalise(norm):
                dve.wait_ge(rstd_done, norm + 1)
                for g in range(G):
                    dve.tensor_scalar(y[:, g, :], x[:, g, :], rstd[:, g:g + 1], None, ALU.mult).then_inc(y_done, 1)

            def mod_shift(l, i, b, c0):
                p0 = l * 48 + 24 * i
                dve.tensor_tensor(mod[:, l, i, 0, :], bank[b][:, c0:c0 + KD], cols1[:, p0:p0 + KD], ALU.add).then_inc(mod_done, 1)

            def mod_gain(l, i, b, c0):
                p0 = l * 48 + 24 * i + KD
                gcol = 96 + 16 * i + 8 * l
                link(dve.tensor_tensor(modt[:, i, :], bank[b][:, c0:c0 + KD], cols1[:, p0:p0 + KD], ALU.add))
                dve.scalar_tensor_tensor(out=mod[:, l, i, 1, :], in0=modt[:, i, :], scalar=1.0,
                                         in1=cols1[:, gcol:gcol + KD], op0=ALU.add, op1=ALU.mult).then_inc(mod_done, 1)

            def gate_half(b, r, gate, half, bias, biases):
                dve.wait_ge(crossed, r + 1)
                dve.wait_ge(bias_in, 16 * biases)
                c = slice(half * 512, (half + 1) * 512)
                dve.tensor_tensor(gate[:, c], bias, bank[b][:, :], ALU.add).then_inc(gate_done, 1)

            vec = [0]

            def sum_unit():
                n = units_of["dve"][vec[0]]
                r, half = vec[0] // 2, vec[0] % 2
                vec[0] += 1
                w = unit_view(n)
                unit_wait(dve, n)
                if r not in IN_FF:
                    dst = ring_sum[:, r % 2, :]
                    if r >= 2 and half == 0:
                        dve.wait_ge(crossed, r - 1)
                else:
                    dst = ff_sum[:, r - IN_FF.start, :]
                for k in range(4):
                    ck = cols2[:, 4 * half + k:4 * half + k + 1]
                    if half == 0 and k == 0:
                        ins = dve.tensor_scalar(dst, w[:, k, :], ck, None, ALU.mult)
                    else:
                        ins = dve.scalar_tensor_tensor(out=dst, in0=w[:, k, :], scalar=ck, in1=dst, op0=ALU.mult, op1=ALU.add)
                    if k < 3:
                        link(ins)
                ins.then_inc(vec_used, 1)
                if half == 0:
                    dve.wait_ge(vec_used, vec[0])

            def add_gated(gate, used, ready, product, halves=(0, 1)):
                for c in halves:
                    for g in range(G):
                        i = 2 * c + g
                        if i in ready:
                            dve.wait_ge(quarter_done, ready[i])
                        else:
                            dve.wait_ge(split_used, used[c])
                        cs = slice(c * 512, (c + 1) * 512)
                        link(dve.tensor_tensor(product(i % 2), bank[4 + i][:, :], gate[:, cs], ALU.mult))
                        dve.tensor_tensor(x[:, g, cs], x[:, g, cs], product(i % 2), ALU.add).then_inc(x_done, 1)

            def rotation_angles():
                dve.wait_ge(pos_in, 16)
                dve.wait_ge(pool_own, 7 + RH)
                link(dve.tensor_copy(pos_f[:, :], pos_i[:, :]))
                for g in range(G):
                    link(dve.tensor_scalar(ang[:, g, :], freq[:, :], pos_f[:, g:g + 1], None, ALU.mult))
                link(dve.tensor_scalar(turns[:, 0, :, :], ang[:, :, :], 1.0 / (2 * np.pi), None, ALU.mult))
                link(dve.tensor_scalar(turns[:, 1, :, :], turns[:, 0, :, :], 0.25, None, ALU.add))
                link(dve.tensor_scalar(turns[:, :, :, :], turns[:, :, :, :], ROUND, None, ALU.add))
                link(dve.tensor_scalar(turns[:, :, :, :], turns[:, :, :, :], -ROUND, None, ALU.add))
                for i in range(2):
                    for j, part in enumerate(TURN):
                        src = ang[:, :, :] if j == 0 else rest[:, i, :, :]
                        link(dve.scalar_tensor_tensor(out=rest[:, i, :, :], in0=turns[:, i, :, :], scalar=-part, in1=src,
                                                      op0=ALU.mult, op1=ALU.add))
                link(dve.tensor_scalar(rest[:, 1, :, :], rest[:, 1, :, :], float(np.pi / 2), None, ALU.add))
                dve.tensor_scalar(rest[:, :, :, :], rest[:, :, :, :], PI_IN, -PI_IN, ALU.min, ALU.max).then_inc(angles, 1)
                dve.wait_ge(trig_done, 1)
                for i in range(2):
                    half = slice(i * RH, (i + 1) * RH)
                    dve.tensor_copy(cos2[:, :, 0, half], trig[:, 1, :, :]).then_inc(trig2, 1)
                    dve.tensor_scalar(sin2[:, :, 0, half], trig[:, 0, :, :], -1.0 if i == 0 else 1.0, None, ALU.mult).then_inc(trig2, 1)

            dve.wait_ge(cols_tp, 1)
            dve.tensor_copy(cols1[:, :], bank[0][:, 0:P]).then_inc(cols_done, 1)
            dve.tensor_copy(cols2[:, 0:30], bank[0][:, P:P + 30]).then_inc(cols_done, 1)
            dve.wait_ge(cols_done, 2)
            for _ in range(4):
                sum_unit()
            variance([(0, 2, D)])
            normalise(0)
            for _ in range(4):
                sum_unit()
            s = 0
            for l in range(L):
                m = ONE_LAYER * l
                RM = 4 if l == 0 else IN_FF.stop
                if l == 0:
                    dve.wait_ge(crossed, 4)
                    mod_shift(0, 0, 4, 0)
                    mod_gain(0, 0, 4, KD)
                    lo(s); s += 1
                    split_operand(m, hf)
                    lo(s); s += 1
                    lo(s); s += 1
                    rotation_angles()
                else:
                    variance([(0, 2, D)])
                    normalise(4 * l)
                    dve.wait_ge(crossed, IN_FF.stop)
                    for i in range(2):
                        mod_shift(1, i, 2, 2 * KD * i)
                        mod_gain(1, i, 2, 2 * KD * i + KD)
                    split_operand(m, hf)
                    lo(s); s += 1
                for _ in range(2):
                    lo(s); s += 1
                    sum_unit()
                variance([(0, 2, QL), (2, 4, KVL)])
                dve.wait_ge(rstd_done, 4 * l + 2)
                if l == 0:
                    dve.wait_ge(trig2, 4)
                for g in range(G):
                    dve.tensor_scalar(lat[:, g, 0:QL], lat[:, g, 0:QL], rstd[:, g:g + 1], None, ALU.mult).then_inc(latn_done, 1)
                    dve.tensor_scalar(lat[:, g, QL:QL + KVL], lat[:, g, QL:QL + KVL], rstd[:, 2 + g:3 + g], None,
                                      ALU.mult).then_inc(latn_done, 1)
                lo(s); s += 1
                sum_unit()
                for g in range(G):
                    kr = lat[:, g, QL + KVL:LAT]
                    ra, rb = rot_a[:, g, 0, :], rot_b[:, g, 0, :]
                    link(dve.tensor_tensor(ra, kr, cos2[:, g, 0, :], ALU.mult))
                    link(dve.tensor_tensor(rb[:, 0:RH], kr[:, RH:RO], sin2[:, g, 0, 0:RH], ALU.mult))
                    link(dve.tensor_tensor(rb[:, RH:RO], kr[:, 0:RH], sin2[:, g, 0, RH:RO], ALU.mult))
                    link(dve.tensor_tensor(kr, ra, rb, ALU.add))
                for g in range(G):
                    dve.tensor_copy(k_tok[:, g, :, HD:QW],
                                    lat[:, g, QL + KVL:LAT].rearrange("p (o c) -> p o c", o=1).to_broadcast([P, H, RO])
                                    ).then_inc(qkrot_done, 1)
                lo(s); s += 1
                sum_unit()
                gate_half(6, RM, gate_m, 0, gate_m[:, 0:512], 2 + l)
                gate_half(7, RM + 1, gate_m, 1, gate_m[:, 512:1024], 2 + l)
                lo(s); s += 1
                if l == 0:
                    sum_unit()
                dve.wait_ge(qtok_done, 4 * (l + 1))
                for g in range(G):
                    qr = q_tok[:, g, :, HD:QW]
                    cb = cos2[:, g, :, :].to_broadcast([P, H, RO])
                    sb0 = sin2[:, g, :, 0:RH].to_broadcast([P, H, RH])
                    sb1 = sin2[:, g, :, RH:RO].to_broadcast([P, H, RH])
                    dve.tensor_tensor(rot_b[:, g, :, 0:RH], qr[:, :, RH:RO], sb0, ALU.mult).then_inc(dve_own, 1)
                    dve.tensor_tensor(rot_b[:, g, :, RH:RO], qr[:, :, 0:RH], sb1, ALU.mult).then_inc(dve_own, 1)
                    own[0] += 2
                    link(dve.tensor_tensor(rot_a[:, g, :, :], qr, cb, ALU.mult))
                    dve.tensor_tensor(qr, rot_a[:, g, :, :], rot_b[:, g, :, :], ALU.add).then_inc(qkrot_done, 1)
                lo(s); s += 1
                if l == 0:
                    sum_unit()
                dve.wait_ge(plain_used, ends["ukv", l])
                for i in range(2):
                    kv = bank[i][:, :].rearrange("p (h c) -> p h c", c=P)
                    dve.tensor_copy(k_tok[:, 1, 4 * i:4 * i + 4, 0:HD], kv[:, :, 0:HD]).then_inc(qkrot_done, 1)
                    dve.tensor_copy(v_mla[:, 1, i * 256:(i + 1) * 256].rearrange("p (h c) -> p h c", c=HD),
                                    kv[:, :, HD:P]).then_inc(vmla_done, 1)
                lo(s); s += 1
                for i in range(1, 8, 2):
                    dve.wait_ge(qk_tp, 8 * l + i + 1)
                    dst = (q_t if i < 4 else k_t)[:, 2 * (i % 4):2 * (i % 4) + 2, :]
                    dve.tensor_copy(dst, bank[(4 + i) % 8][0:QW, :].rearrange("p (h t) -> p h t", t=T)).then_inc(qt_dve, 1)

                for i in range(6 + 2):
                    if 1 <= i <= 6:
                        j = i - 1
                        t = 6 * l + j
                        dve.wait_ge(ln_done, t + 1)
                        kb = keep[:, j if j < 2 else 2 + j % 2, :]
                        dve.scalar_tensor_tensor(out=kb, in0=zm[:, j % 3, :], scalar=0.0, in1=kb, op0=ALU.max,
                                                 op1=ALU.add).then_inc(keep_done, 1)
                    if i >= 2:
                        j = i - 2
                        t = 6 * l + j
                        dve.wait_ge(cs_ready, t + 1)
                        dve.tensor_tensor(zm[:, j % 3, :], zm[:, j % 3, :], bank[1][:, :],
                                          ALU.subtract).then_inc(w_done, 1)
                    if i < 6:
                        t = 6 * l + i
                        dve.wait_ge(z_ready, t + 1)
                        if i >= 3:
                            dve.wait_ge(stick_done, t - 2)
                        w = P if i < 2 else T
                        n = 512 // w
                        dve.tensor_tensor(zm[:, i % 3, :].rearrange("p (h q) -> p h q", q=w),
                                          bank[0][:, :].rearrange("p (h q) -> p h q", q=w),
                                          strict[:, 0:w].rearrange("p (o q) -> p o q", o=1).to_broadcast([P, n, w]),
                                          ALU.add).then_inc(zm_done, 1)
                        dve.wait_ge(s_ready, t + 1)
                        if i >= 2:
                            dve.wait_ge(p_tp, t - 1)
                        heads = 4 if i < 2 else 2
                        w = 512 // heads
                        c0 = 4 * i if i < 2 else H + 2 * (i - 2)
                        pr = probs[:, i % 2, :].rearrange("p (h k) -> p h k", k=w)
                        mk = chunked[:, T - w:T].rearrange("p (o k) -> p o k", o=1).to_broadcast([P, heads, w])
                        link(dve.tensor_tensor(pr, bank[4][:, :].rearrange("p (h k) -> p h k", k=w), mk, ALU.add))
                        dve.tensor_reduce(neg_max[:, c0:c0 + heads], pr, AX.X, ALU.max, negate=True).then_inc(max_done, 1)
                    if i == 3:
                        lo(s); s += 1
                    if i < 2 and l == 0:
                        sum_unit()
                    if i == 3 and l == 0:
                        dve.wait_ge(crossed, 8)
                        mod_shift(0, 1, 7, 0)
                    if 1 <= i <= 6:
                        j = i - 1
                        t = 6 * l + j
                        dve.wait_ge(p_tp, t + 1)
                        if j >= 2:
                            dve.wait_ge(mpv_done, t - 1)
                        dve.tensor_copy(probs_t[:, j % 2, :], bank[5][:, :]).then_inc(pt_done, 1)
                dve.wait_ge(p_done, 16 * (l + 1))
                link(dve.reciprocal(recip[:, :], sums[:, :]))
                dve.wait_ge(mpv_done, 6 * (l + 1))
                for g in range(G):
                    dve.tensor_tensor(y[:, g, 0:MW].rearrange("p (h c) -> p h c", c=HD),
                                      bank[6 + g][:, :].rearrange("p (h c) -> p h c", c=HD),
                                      recip[:, g * H:(g + 1) * H].rearrange("p (h o) -> p h o", o=1).to_broadcast([P, H, HD]),
                                      ALU.mult).then_inc(omla_done, 1)
                dve.wait_ge(pv_done, 6 * (l + 1))
                for g in range(G):
                    dve.tensor_copy(y[:, g, MW:], bank[2 + g][:, :]).then_inc(osb_done, 1)
                variance([(0, 4, MW)])
                dve.wait_ge(rstd_done, 4 * l + 3)
                for g in range(G):
                    for i in range(2):
                        part = y[:, g, i * 512:(i + 1) * 512]
                        dve.tensor_scalar(part, part, rstd[:, 2 * g + i:2 * g + i + 1], None, ALU.mult).then_inc(y_done, 1)
                split_operand(m + 1, hf)
                sum_unit()
                sum_unit()
                lo(s); s += 1
                sum_unit()
                sum_unit()
                dve.wait_ge(gate_done, 2 if l == 0 else 6)
                for c in range(2):
                    add_gated(gate_m, (ends["out", l, 0], ends["out", l, 1]), {0: 5 * l + 1, 2: 5 * l + 2},
                              lambda i: probs[:, i, :], (c,))
                    if (l, c) == (0, 0):
                        dve.wait_ge(crossed, 10)
                        mod_gain(0, 1, 0, 0)
                if l == 1:
                    for half in range(2):
                        gate_half(half, RM + 2 + half, gate_f, half, gate_f[:, half * 512:(half + 1) * 512], 4)
                variance([(0, 2, D)])
                normalise(4 * l + 3)
                if l == 0:
                    lo(s); s += 1
                    split_operand(m + 2, hfn)
                    lo(s); s += 1
                    lo(s); s += 1
                    def gated_ff(c):
                        dve.wait_ge(silu_done, 2 * c + 2)
                        dve.wait_ge(split_used, ends["up", c])
                        for i in range(2):
                            link(dve.tensor_tensor(act[:, 2 * i:2 * i + 2, :], act[:, 2 * i:2 * i + 2, :],
                                                   bank[2 + i][:, :].rearrange("p (k t) -> p k t", t=T), ALU.mult))
                        if c >= 2:
                            dve.wait_ge(split_used, ends["down", c - 2])
                        dve.tensor_copy(a_hi[:, c % 2, :, :], act[:, :, :]).then_inc(a_done, 1)
                        dve.wait_ge(a_done, 2 * c + 1)
                        dve.tensor_tensor(a_lo[:, c % 2, :, :], act[:, :, :], a_hi[:, c % 2, :, :].bitcast(F32),
                                          ALU.subtract).then_inc(a_done, 1)

                    for j, (kind, c, half) in enumerate(ff_order):
                        if j >= FF_FIRST:
                            lo(s); s += 1
                        for _ in range(ff_ada.get(j, 0)):
                            sum_unit()
                        if (kind, c, half) == ("gate", 1, 1):
                            gated_ff(0)
                        if (kind, half) == ("down", 1) and c + 1 < FC:
                            gated_ff(c + 1)
                    for half in range(2):
                        gate_half(half, 10 + half, gate_f, half, gate_f[:, half * 512:(half + 1) * 512], 2)
                    lo(s); s += 1
                    lo(s); s += 1
                    dve.wait_ge(gate_done, 4)
                    add_gated(gate_f, (ends["down", FC - 1],) * 2, {0: 3, 1: 4, 2: 5},
                              lambda i: act[:, 2 * i:2 * i + 2, :].rearrange("p a t -> p (a t)"))

            dve.wait_ge(router_in, 32)
            dve.wait_ge(lgt_ready, 1)
            dve.tensor_copy(logits_t[:, :], bank[4][0:E, 0:T]).then_inc(lgt_done, 1)
            dve.wait_ge(lg_ready, 1)
            link(dve.tensor_tensor(logits[:, :, :], bank[6][:, 0:G * E].rearrange("p (g e) -> p g e", e=E),
                                   br[:, :].rearrange("p (o e) -> p o e", o=1).to_broadcast([P, G, E]), ALU.add))
            for g in range(G):
                ins = dve.max(top[:, g, :], logits[:, g, :])
                own[0] += 1
                ins.then_inc(dve_own, 1)
            dve.wait_ge(dve_own, own[0])
            for g in range(G):
                ins = dve.max_index(topi[:, g, :], top[:, g, :], logits[:, g, :])
                own[0] += 1
                ins.then_inc(dve_own, 1)
            dve.tensor_tensor(tw[:, :, 0], top[:, :, 1], top[:, :, 0], ALU.subtract).then_inc(rd_done, 1)
            dve.wait_ge(dve_own, own[0])
            link(dve.tensor_copy(topf[:, :, :], topi[:, :, :]))
            for g in range(G):
                for i in range(2):
                    ins = dve.tensor_scalar(hot[:, g, i, :], slot_no[:, 0:E], topf[:, g, i:i + 1], None, ALU.is_equal)
                    own[0] += 1
                    ins.then_inc(dve_own, 1)
            dve.wait_ge(dve_own, own[0])
            dve.tensor_tensor(chosen[:, :, :], hot[:, :, 0, :], hot[:, :, 1, :], ALU.add).then_inc(ch_done, 1)
            dve.wait_ge(re_done, 1)
            link(dve.tensor_scalar(tw[:, :, 2], tw[:, :, 1], 1.0, None, ALU.add))
            link(dve.reciprocal(tw[:, :, 2], tw[:, :, 2]))
            link(dve.tensor_tensor(tw[:, :, 3], tw[:, :, 1], tw[:, :, 2], ALU.mult))
            for g in range(G):
                link(dve.tensor_scalar(comb[:, g, :], hot[:, g, 0, :], tw[:, g, 2:3], None, ALU.mult))
                link(dve.scalar_tensor_tensor(out=comb[:, g, :], in0=hot[:, g, 1, :], scalar=tw[:, g, 3:4],
                                              in1=comb[:, g, :], op0=ALU.mult, op1=ALU.add))
            dve.wait_ge(pos_ready, 1)
            by_expert = lambda t: t.rearrange("p g e -> p e g")
            slots = place[:, 0:E, 0:G]
            link(dve.scalar_tensor_tensor(out=slots, in0=by_expert(chosen[:, :, :]), scalar=-ABSENT,
                                          in1=bank[5][:, 0:G * E].rearrange("p (g e) -> p e g", g=G),
                                          op0=ALU.mult, op1=ALU.add))
            link(dve.tensor_scalar(slots, slots, ABSENT, None, ALU.add))

            def select(slot):
                for g in range(G):
                    dve.tensor_scalar(sel[:, g, :], slot_no[:, :], slot[:, g:g + 1], None, ALU.is_equal).then_inc(sel_done, 1)

            def low_rows(i, done):
                c = slice(i * 512, (i + 1) * 512)
                dve.tensor_tensor(ye_lo[:, c], bank[4 + i][:, :], ye_hi[:, c].bitcast(F32), ALU.subtract).then_inc(done, 1)

            def add_rows(i, done):
                g, half = i // 2, i % 2
                a = acc[:, g, half * 512:(half + 1) * 512]
                dve.scalar_tensor_tensor(out=a, in0=bank[6 + i % 2][:, :], scalar=w_before[:, g:g + 1], in1=a,
                                         op0=ALU.mult, op1=ALU.add).then_inc(done, 1)

            def split_gathered(q):
                for i in range(2):
                    dve.wait_ge(hgf_done, q * KD + (4 * i + 4))
                    part = slice(4 * i, 4 * i + 4)
                    dve.tensor_copy(hg_hi[:, part, :], hgf[:, part, :]).then_inc(hg_done, 1)
                    dve.wait_ge(hg_done, q * 4 + (2 * i + 1))
                    dve.tensor_tensor(hg_lo[:, part, :], hgf[:, part, :], hg_hi[:, part, :].bitcast(F32),
                                      ALU.subtract).then_inc(hg_done, 1)

            link(dve.tensor_reduce(full[:, :], bank[5][:, 2 * E:3 * E], AX.X, ALU.max))
            select(place[:, 0, :])
            link(dve.tensor_scalar(place[:, E:2 * E, 0:G], slots, float(-P), None, ALU.add))
            for r in range(2):
                link(dve.tensor_copy(place[:, r * E:(r + 1) * E, 2:2 + G], by_expert(comb[:, :, :])))
            link(dve.memset(place[:, 2 * E, :], ABSENT))
            link(dve.tensor_copy(now[:, :], place[:, 0, :]))
            dve.tensor_scalar(sel_t[:, :], strict[:, :], 0.0, None, ALU.mult).then_inc(sw_done, 1)
            link(dve.memset(w_before[:, :], 0.0))
            dve.tensor_copy(full_i[:, :], full[:, :]).then_inc(place_done, 1)
            base = own[0]
            dve.wait_ge(acc_zero, 1)

            def expert(q):
                def lo_e(j):
                    dve.wait_ge(hi_done, q * NU + (S0 + j + 1))
                    sl = (S0 + j) % SPLIT
                    dve.tensor_tensor(w_lo[:, sl, :], raw[:, (N0 + j) % RAW, :], w_hi[:, sl, :].bitcast(F32),
                                      ALU.subtract).then_inc(lo_done, 1)

                def gated(c):
                    dve.wait_ge(esilu, q * EC + (c + 1))
                    dve.wait_ge(split_used, q * NU + (S0 + at["up", c, 1] + 1))
                    dve.tensor_tensor(e_act[:, :], e_act[:, :], bank[1][:, :], ALU.mult).then_inc(ea_done, 1)

                def low_t(c):
                    dve.wait_ge(ehi_done, q * EC + (c + 1))
                    dve.tensor_tensor(e_lo[:, c % 2, :, :], bank[2][:, :].rearrange("p (k t) -> p k t", t=P),
                                      e_hi[:, c % 2, :, :].bitcast(F32), ALU.subtract).then_inc(elo_done, 1)

                for j, (kind, c, half) in enumerate(order):
                    lo_e(j)
                    if (kind, c, half) == ("gate", 0, 0):
                        split_gathered(q)
                    if (kind, c, half) == ("gate", 0, 1):
                        for i in range(2):
                            dve.wait_ge(ye_done, q * 2 + (i + 1))
                            low_rows(i, yl_done)
                    if (kind, c, half) == ("up", 0, 0):
                        for i in range(4):
                            dve.wait_ge(sc_ready, q * 4 + (i + 1))
                            add_rows(i, acc_done)
                    if (kind, half) == ("up", 1) and c > 0:
                        low_t(c - 1)
                    if (kind, c, half) == ("gate", 1, 1):
                        gated(0)
                    if (kind, c, half) == ("down", 3, 1):
                        dve.wait_ge(acc_done, q * 4 + 4)
                        dve.tensor_copy(w_before[:, :], now[:, 2:4]).then_inc(dve_own, 1)
                        dve.wait_ge(dve_own, q * 2 + (base + 1))
                        dve.tensor_copy(now[:, :], place[:, bass.ds(q + 1, 1), :]).then_inc(dve_own, 1)
                        dve.wait_ge(dve_own, q * 2 + (base + 2))
                        select(now)
                    if (kind, half) == ("down", 1) and c + 1 < EC:
                        gated(c + 1)
                    if (kind, c, half) == ("down", EC - 1, 0):
                        low_t(EC - 1)

            with dve.Fori(0, E) as q:
                expert(q)
            dve.wait_ge(place_done, 1)
            more = dve.value_load(full_i[0:1, 0:1])
            with dve.If(more > P):
                with dve.Fori(E, 2 * E) as q:
                    expert(q)
                dve.wait_ge(acc_done, 8 * E)
            dve.wait_ge(acc_done, 4 * E)
            dve.wait_ge(gate_done, 8)
            gb = gate_f[:, :].rearrange("p (o d) -> p o d", o=1).to_broadcast([P, G, D])
            dve.tensor_tensor(acc[:, :, :], acc[:, :, :], gb, ALU.mult).then_inc(fin_acc, 1)
            dve.wait_ge(fin_acc, 1)
            dve.tensor_tensor(x[:, :, :], x[:, :, :], acc[:, :, :], ALU.add).then_inc(fin_acc, 1)
            dve.wait_ge(fin_acc, 2)
            for i in range(2):
                dve.wait_ge(ye_end, i + 1)
                low_rows(i, yl_end)
            for i in range(4):
                g, half = i // 2, i % 2
                cs = slice(half * 512, (half + 1) * 512)
                dve.wait_ge(sc_end, i + 1)
                dve.scalar_tensor_tensor(out=acc[:, g, cs], in0=bank[6 + i % 2][:, :], scalar=w_before[:, g:g + 1],
                                         in1=gate_f[:, cs], op0=ALU.mult, op1=ALU.mult).then_inc(acc_end, 1)
                dve.wait_ge(acc_end, i + 1)
                dve.tensor_tensor(x[:, g, cs], x[:, g, cs], acc[:, g, cs], ALU.add).then_inc(fin_x, 1)
            variance([(0, 2, D)])
            dve.wait_ge(rstd_done, 4 * L + 1)
            dve.wait_ge(final_in, 16)
            for g in range(G):
                dve.scalar_tensor_tensor(out=y[:, g, :], in0=x[:, g, :], scalar=rstd[:, g:g + 1], in1=final_gain[:, :],
                                         op0=ALU.mult, op1=ALU.mult).then_inc(fin_y, 1)

        @block.tensor
        def _(pe):
            mm = pe.matmul

            def product(o, lh, ll, rh, rl, first, last):
                mm(o, lh, rh, start=first, stop=False, skip_group_check=True)
                mm(o, lh, rl, start=False, stop=False, skip_group_check=True)
                return mm(o, ll, rh, start=False, stop=last, skip_group_check=True)

            plain = [0]

            def plain_unit():
                n = units_of["pe"][plain[0]]
                plain[0] += 1
                unit_wait(pe, n)
                return unit_view(n)

            def across(r, b, c0=None):
                pe.wait_ge(vec_used, 2 * r + 2)
                src = ff_sum[:, r - IN_FF.start, :] if r in IN_FF else ring_sum[:, r % 2, :]
                if c0 is None:
                    last = mm(bank[b][:, :], ones[:, :], src, start=True, stop=True)
                else:
                    for j in range(4):
                        last = mm(bank[b][:, c0 + j:c0 + j + 1], src[:, j * P:(j + 1) * P], ones[:, 0:1], start=True,
                                  stop=True, skip_group_check=True)
                last.then_inc(crossed, 1)

            s = [0]

            def split_unit():
                n = units_of["split"][s[0]]
                _, k, cols, _ = stream[n]
                sl = s[0] % SPLIT
                s[0] += 1
                pe.wait_ge(lo_done, s[0])
                f = lambda w: w[:, sl, 0:k * cols].rearrange("p (k n) -> p k n", k=k)
                return f(w_hi), f(w_lo)

            def transposes(m, ready):
                pe.wait_ge(y_done, ready)
                for j in range(4):
                    for a in range(2):
                        for g in range(G):
                            k = 2 * j + a
                            last = pe.transpose(bank[j][:, a * T + g * P:a * T + (g + 1) * P], y[:, g, k * P:(k + 1) * P],
                                                ident[:, :])
                    last.then_inc(h_tp, 1)

            def operand_slices(m, kk):
                if m is not None and kk % 2 == 0:
                    pe.wait_ge(h_done, 8 * m + kk + 2)

            def rows_product(banks, cols, m=None, by_group=False):
                for half in range(2):
                    wh, wl = split_unit()
                    for g in range(G):
                        for k in range(4):
                            kk = 4 * half + k
                            if g == 0:
                                operand_slices(m, kk)
                            last = product(bank[banks + g][:, 0:cols], h_hi[:, kk, g * P:(g + 1) * P],
                                           h_lo[:, kk, g * P:(g + 1) * P], wh[:, k, :], wl[:, k, :], kk == 0, kk == 7)
                        if by_group and (half, g) == (1, 0):
                            last.then_inc(quarter_done, 1)
                    last.then_inc(split_used, 1)

            def columns_half(b0, half, m=None):
                wh, wl = split_unit()
                for j in range(4):
                    for k in range(4):
                        kk = 4 * half + k
                        if j == 0:
                            operand_slices(m, kk)
                        o = bank[b0 + j // 2][:, (j % 2) * T:(j % 2 + 1) * T]
                        js = slice(j * P, (j + 1) * P)
                        last = product(o, wh[:, k, js], wl[:, k, js], h_hi[:, kk, :], h_lo[:, kk, :],
                                       kk == 0 and j % 2 == 0, kk == 7)
                last.then_inc(split_used, 1)

            def columns_product(b0, m=None):
                columns_half(b0, 0, m)
                columns_half(b0, 1, m)

            pe.wait_ge(consts, 5)
            pe.wait_ge(c_silu, 1)
            pe.wait_ge(small_in, 16 * 8)
            pe.transpose(bank[0][:, 0:P], rows1[:, :], ident[:, :])
            pe.transpose(bank[0][:, P:P + 30], rows2[0:30, :], ident[0:30, 0:30]).then_inc(cols_tp, 1)
            pe.wait_ge(cols_done, 2)
            across(0, 4, 0)
            across(1, 4, 4)
            transposes(0, 2)
            across(2, 4, 8)
            across(3, 4, 12)
            normed = 0
            for l in range(L):
                m = ONE_LAYER * l
                RM = 4 if l == 0 else IN_FF.stop
                normed += 2
                if l > 0:
                    for n in range(8):
                        across(12 + n, 2, 4 * n)
                    pe.wait_ge(mod_done, 8)
                    transposes(m, normed)
                rows_product(0, LAT, m)
                rows_product(2, 512)
                columns_half(4, 0)
                across(RM, 6)
                pe.wait_ge(latn_done, 4 * (l + 1))
                pe.wait_ge(lat_done, 2 * (l + 1))
                for b in range(3):
                    for g in range(G):
                        o = bank[0][:, b * T + g * P:b * T + (g + 1) * P] if b < 2 else bank[1][:, g * P:(g + 1) * P]
                        last = pe.transpose(o, lat[:, g, b * P:(b + 1) * P], ident[:, :])
                    if b > 0:
                        last.then_inc(lat_tp, 1)
                columns_half(4, 1)
                uq = plain_unit()
                pe.wait_ge(latt_done, 3 * (l + 1))
                pe.wait_ge(vsb_done, 2 * (l + 1))
                for g in range(G):
                    bq = 2 if g == 0 else 0
                    for i, (a, w) in enumerate(((0, 5 * QW), (5 * QW, 3 * QW))):
                        for k in range(2):
                            last = mm(bank[bq + i][:, 0:w], lat_t[:, k, g * P:(g + 1) * P], uq[:, k, a:a + w],
                                      start=k == 0, stop=k == 1)
                last.then_inc(plain_used, 1)
                across(RM + 1, 7)
                pe.wait_ge(gate_done, 2 if l == 0 else 6)
                columns_half(6, 0)
                ukv = plain_unit()
                pe.wait_ge(qtok_done, 4 * (l + 1))
                for g in range(G):
                    bk = 2 if g == 0 else 0
                    for i in range(2):
                        last = mm(bank[bk + i][:, :], lat_t[:, 2, g * P:(g + 1) * P], ukv[:, 0, i * 512:(i + 1) * 512],
                                  start=True, stop=True)
                last.then_inc(plain_used, 1)
                columns_half(6, 1)
                for i in range(8):
                    src = q_tok if i < 4 else k_tok
                    if i == 0:
                        pe.wait_ge(qkrot_done, 6 * l + 4)
                        pe.wait_ge(qk_done, 4 * l + 2)
                    if i == 2:
                        pe.wait_ge(qk_done, 4 * l + 4)
                    if i == 4:
                        pe.wait_ge(qkrot_done, 6 * l + 6)
                        pe.wait_ge(vmla_done, 2 * (l + 1))
                        pe.wait_ge(kv_act, 4 * (l + 1))
                    for a in range(2):
                        for g in range(G):
                            last = pe.transpose(bank[(4 + i) % 8][0:QW, a * T + g * P:a * T + (g + 1) * P],
                                                src[:, g, 2 * (i % 4) + a, :], ident[:, :])
                    last.then_inc(qk_tp, 1)
                pe.wait_ge(qt_act, 4 * (l + 1))
                pe.wait_ge(qt_dve, 4 * (l + 1))
                if l == 0:
                    across(6, 7, 0)

                for i in range(6 + 3):
                    t = 6 * l + i
                    if i < 6:
                        if i >= 1:
                            pe.wait_ge(zm_done, t)
                        for a, h in enumerate(sb_heads(i)):
                            pp = slice((h % 2) * HD, (h % 2 + 1) * HD)
                            kb, qs, w = (1, slice(P, T), P) if i < 2 else (0, slice(0, T), T)
                            last = mm(bank[0][:, a * w:(a + 1) * w], k_sbt[pp, h // 2, kb * P:(kb + 1) * P],
                                      q_sbt[pp, h // 2, qs], start=(a == 0), stop=True, skip_group_check=True)
                        last.then_inc(z_ready, 1)
                        if i >= 1:
                            pe.wait_ge(max_done, t)
                        for a in range(4 if i < 2 else 2):
                            h = 4 * i + a if i < 2 else 2 * (i - 2) + a
                            g, w = (0, P) if i < 2 else (1, T)
                            last = mm(bank[4][:, a * w:(a + 1) * w], q_t[:, h, g * P:(g + 1) * P], k_t[:, h, 0:w],
                                      start=(a == 0), stop=True, skip_group_check=True)
                        last.then_inc(s_ready, 1)
                    if l == 0 and i == 3:
                        across(7, 7, 4)
                    if 1 <= i <= 6:
                        j = i - 1
                        t = 6 * l + j
                        pe.wait_ge(keep_done, t + 1)
                        if j >= 1:
                            pe.wait_ge(w_done, t)
                        kb = keep[:, j if j < 2 else 2 + j % 2, :]
                        last = mm(bank[1][:, :], from_here[:, :], kb, start=True, stop=j < 2, skip_group_check=True)
                        if j >= 2:
                            for a, h in enumerate(sb_heads(j)):
                                last = mm(bank[1][:, a * T + P:(a + 1) * T], ones[:, :],
                                          keep[:, h % 2, (h // 2) * P:(h // 2 + 1) * P], start=False, stop=a == 1,
                                          skip_group_check=True)
                        last.then_inc(cs_ready, 1)
                        pe.wait_ge(p_done, 16 * l + (4 * (j + 1) if j < 2 else 8 + 2 * (j - 1)))
                        if j >= 1:
                            pe.wait_ge(pt_done, t)
                        for a in range(4):
                            last = pe.transpose(bank[5][:, a * P:(a + 1) * P], probs[:, j % 2, a * P:(a + 1) * P],
                                                ident[:, :])
                        last.then_inc(p_tp, 1)
                    if 2 <= i <= 7:
                        j = i - 2
                        t = 6 * l + j
                        pe.wait_ge(pt_done, t + 1)
                        if l == 0 and j == 2:
                            pe.wait_ge(mod_done, 3)
                        for a in range(4):
                            if j < 2:
                                h, g, kb = 4 * j + a, 0, 0
                            else:
                                h, g, kb = 2 * (j - 2) + a // 2, 1, a % 2
                            last = mm(bank[6 + g][:, h * HD:(h + 1) * HD], probs_t[:, j % 2, a * P:(a + 1) * P],
                                      v_mla[:, kb, h * HD:(h + 1) * HD], start=(h == 0 and kb == 0), stop=(kb == g),
                                      skip_group_check=True)
                        last.then_inc(mpv_done, 1)
                    if i >= 3:
                        j = i - 3
                        t = 6 * l + j
                        pe.wait_ge(stick_done, t + 1)
                        for a, h in enumerate(sb_heads(j)):
                            if j < 2:
                                last = mm(bank[3][:, h * HD:(h + 1) * HD], sticks[:, j % 2, a * P:(a + 1) * P],
                                          v_sb[:, 1, h * HD:(h + 1) * HD], start=(j == 0 and a == 0), stop=False,
                                          skip_group_check=True)
                            else:
                                for g in range(G):
                                    last = mm(bank[2 + g][:, h * HD:(h + 1) * HD],
                                              sticks[:, j % 2, a * T + g * P:a * T + (g + 1) * P],
                                              v_sb[:, 0, h * HD:(h + 1) * HD], start=(j == 2 and a == 0 and g == 0),
                                              stop=True, skip_group_check=True)
                        last.then_inc(pv_done, 1)
                normed += 4
                transposes(m + 1, normed)
                rows_product(4, 512, m + 1, by_group=True)
                rows_product(6, 512, by_group=True)
                if l == 0:
                    across(8, 0, 0)
                    across(9, 0, 4)
                    pe.wait_ge(mod_done, 4)
                else:
                    across(RM + 2, 0)
                    across(RM + 3, 1)
                    pe.wait_ge(gate_done, 8)
                normed += 2
                transposes(m + 2, normed)
                if l == 0:
                    for c in range(FC + 1):
                        if c < FC:
                            if c > 0:
                                pe.wait_ge(silu_done, 2 * c)
                            columns_product(0, m + 2 if c == 0 else None)
                            if c > 0:
                                pe.wait_ge(a_done, 2 * c)
                            columns_product(2)
                        if c > 0:
                            pe.wait_ge(a_done, 2 * c)
                            cc = c - 1
                            for pair in range(2):
                                if c == FC and pair == 1:
                                    pe.wait_ge(silu_done, 2 * FC)
                                    across(10, 0)
                                    across(11, 1)
                                wh, wl = split_unit()
                                for half in range(2):
                                    for g in range(G):
                                        for k in range(2):
                                            kk = 2 * pair + k
                                            cs = slice(half * 512, (half + 1) * 512)
                                            ts = slice(g * P, (g + 1) * P)
                                            last = product(bank[4 + 2 * half + g][:, :], a_hi[:, cc % 2, kk, ts],
                                                           a_lo[:, cc % 2, kk, ts], wh[:, k, cs], wl[:, k, cs],
                                                           cc == 0 and kk == 0, cc == FC - 1 and kk == 3)
                                        if (c, pair) == (FC, 1) and (half, g) != (1, 1):
                                            last.then_inc(quarter_done, 1)
                                last.then_inc(split_used, 1)

            pe.wait_ge(router_in, 32)
            pe.wait_ge(hf_done, KD * L * ONE_LAYER)
            for k in range(KD):
                last = mm(bank[4][0:E, 0:T], wr[:, k, :], hfm[:, k, :], start=k == 0, stop=k == KD - 1)
            last.then_inc(lgt_ready, 1)
            pe.wait_ge(lgt_done, 1)
            for g in range(G):
                last = pe.transpose(bank[6][:, g * E:(g + 1) * E], logits_t[:, g * P:(g + 1) * P], ident[0:E, 0:E])
            last.then_inc(lg_ready, 1)
            pe.wait_ge(ch_done, 1)
            o = lambda i: bank[5][:, i * E:(i + 1) * E]
            mm(o(0), before[:, :], chosen[:, 0, :], start=True, stop=True, skip_group_check=True)
            mm(o(1), before[:, :], chosen[:, 1, :], start=False, stop=False, skip_group_check=True)
            mm(o(1), ones[:, :], chosen[:, 0, :], start=False, stop=True, skip_group_check=True)
            mm(o(2), ones[:, :], chosen[:, 0, :], start=False, stop=False, skip_group_check=True)
            mm(o(2), ones[:, :], chosen[:, 1, :], start=False, stop=True, skip_group_check=True).then_inc(pos_ready, 1)

            def gather(q):
                pe.wait_ge(sel_done, q * 2 + 2)
                for k in range(KD):
                    for g in range(G):
                        last = mm(bank[6 + k // 4][:, (k % 4) * P:(k % 4 + 1) * P], y[:, g, k * P:(k + 1) * P], sel[:, g, :],
                                  start=(k % 4 == 0 and g == 0), stop=g == 1, skip_group_check=True)
                    if k % 4 == 3:
                        last.then_inc(hg_ready, 1)

            def selection_t(q):
                for g in range(G):
                    last = pe.transpose(bank[3][:, g * P:(g + 1) * P], sel[:, g, :], ident[:, :])
                last.then_inc(sw_tp, 1)

            def scatter(i, done):
                g, half = i // 2, i % 2
                for part in (ye_hi, ye_lo):
                    last = mm(bank[6 + i % 2][:, :], sel_t[:, g * P:(g + 1) * P], part[:, half * 512:(half + 1) * 512],
                              start=part is ye_hi, stop=part is ye_lo, skip_group_check=True)
                last.then_inc(done, 1)

            gather(0)

            def expert(q):
                def unit(kind, c, half):
                    j = at[(kind, c, half)]
                    pe.wait_ge(lo_done, q * NU + (S0 + j + 1))
                    sl = (S0 + j) % SPLIT
                    k = 2 if kind == "down" else 4
                    f = lambda w: w[:, sl, :].rearrange("p (k n) -> p k n", k=k)
                    return f(w_hi), f(w_lo)

                def into(kind, c, b):
                    for half in range(2):
                        wh, wl = unit(kind, c, half)
                        if (kind, c) == ("gate", 0):
                            pe.wait_ge(hg_done, q * 4 + (2 * half + 2))
                        for k in range(4):
                            kk = 4 * half + k
                            last = product(bank[b][:, :], hg_hi[:, kk, :], hg_lo[:, kk, :], wh[:, k, :], wl[:, k, :],
                                           kk == 0, kk == 7)
                        last.then_inc(split_used, 1)

                def act_t(c):
                    pe.wait_ge(ea_done, q * EC + (c + 1))
                    if c > 0:
                        pe.wait_ge(elo_done, q * EC + c)
                    for a in range(4):
                        last = pe.transpose(bank[2][:, a * P:(a + 1) * P], e_act[:, a * P:(a + 1) * P], ident[:, :])
                    last.then_inc(e_tp, 1)

                def down(c, pair):
                    pe.wait_ge(elo_done, q * EC + (c + 1))
                    wh, wl = unit("down", c, pair)
                    for half in range(2):
                        for k in range(2):
                            kk = 2 * pair + k
                            cs = slice(half * 512, (half + 1) * 512)
                            last = product(bank[4 + half][:, :], e_hi[:, c % 2, kk, :], e_lo[:, c % 2, kk, :],
                                           wh[:, k, cs], wl[:, k, cs], c == 0 and kk == 0, c == EC - 1 and kk == 3)
                    last.then_inc(split_used, 1)

                for c in range(EC):
                    if c > 0:
                        pe.wait_ge(esilu, q * EC + c)
                    into("gate", c, 0)
                    if c == 0:
                        pe.wait_ge(yl_done, q * 2 + 2)
                        pe.wait_ge(sw_done, q + 1)
                        for i in range(4):
                            if i >= 2:
                                pe.wait_ge(acc_done, q * 4 + (i - 1))
                            scatter(i, sc_ready)
                        selection_t(q)
                    else:
                        act_t(c - 1)
                        pe.wait_ge(ea_done, q * EC + c)
                    into("up", c, 1)
                    if c > 0:
                        down(c - 1, 0)
                        if c == EC - 1:
                            act_t(EC - 1)
                        down(c - 1, 1)
                    if c == EC - 2:
                        pe.wait_ge(acc_done, q * 4 + 4)
                        gather(q + 1)
                down(EC - 1, 0)
                down(EC - 1, 1)

            with pe.Fori(0, E) as q:
                expert(q)
            pe.wait_ge(place_done, 1)
            more = pe.value_load(full_i[0:1, 0:1])
            with pe.If(more > P):
                with pe.Fori(E, 2 * E) as q:
                    expert(q)
                pe.wait_ge(sw_done, 2 * E + 1)
            pe.wait_ge(sw_done, E + 1)
            pe.wait_ge(yl_end, 2)
            for i in range(4):
                if i >= 2:
                    pe.wait_ge(acc_end, i - 1)
                scatter(i, sc_end)


_INS = ["x", "c", "positions", "w_ada", "b_ada", "g_mix", "g_ffn", "w_in", "g_q_lat", "w_uq", "g_kv_lat", "w_ukv",
        "g_grp_mla", "g_grp_sb", "w_out", "w_ff_gate", "w_ff_up", "w_ff_down", "w_router", "b_router", "w_ex_gate",
        "w_ex_up", "w_ex_down", "g_final"]


def kernel(**inputs):
    import concourse.bacc as bacc
    from concourse.bass_utils import run_bass_kernel_spmd

    nc = bacc.Bacc("TRN2", target_bir_lowering=False, num_devices=1)
    arrays, args = {}, []
    for name in _INS:
        a = np.ascontiguousarray(inputs[name])
        arrays[f"in_{name}"] = a
        args.append(nc.dram_tensor(f"in_{name}", a.shape, mybir.dt.from_np(a.dtype), kind="ExternalInput").ap())
    shape = inputs["x"].shape
    out = nc.dram_tensor("out_trunk", shape, F32, kind="ExternalOutput").ap()
    trunk_kernel(nc, *args, out)
    r = run_bass_kernel_spmd(nc, [arrays], core_ids=[0])
    return r.results[0]["out_trunk"]
```
